# Optimizing a Trainium2 kernel written in Bass

```python
import math
import jax
import jax.numpy as jnp
from jax import lax
import numpy as np
import jax, jax.numpy as jnp

D_MODEL = 1024
BATCH = 1
SEQ = 256
DEPTH = 2

CHUNK = 64

D_A = D_MODEL // 2
S5_H = 16
S5_G = D_A // S5_H
S5_P = 64
DT_MIN = 1e-3
DT_MAX = 1e-1
D_B = D_MODEL - D_A
POOL_WINDOWS = (2, 4, 8, 16)
POOL_GROUPS = len(POOL_WINDOWS)
POOL_C = D_B // POOL_GROUPS
SB_HEADS = 16
SB_HEAD_DIM = D_MODEL // SB_HEADS
SB_BLOCK = 128
N_EXPERTS = 16
N_EXPERT_GROUPS = 4
EXPERTS_PER_GROUP = N_EXPERTS // N_EXPERT_GROUPS
TOP_K = 2
D_EXPERT = 512
PLE_DIM = 256
DEEPNORM_ALPHA = (2 * DEPTH) ** 0.25
DEEPNORM_BETA = (8 * DEPTH) ** -0.25
LN_EPS = 1e-5
N_EVEN = (DEPTH + 1) // 2
N_ODD = DEPTH // 2


F32 = jnp.float32

def layer_norm(x, g, b):
    x32 = x.astype(F32)
    mu = jnp.mean(x32, axis=-1, keepdims=True)
    var = jnp.mean(jnp.square(x32 - mu), axis=-1, keepdims=True)
    return ((x32 - mu) * lax.rsqrt(var + LN_EPS) * g.astype(F32) + b.astype(F32)).astype(x.dtype)

def _complex_linear_combine(e1, e2):
    a1r, a1i, b1r, b1i = e1
    a2r, a2i, b2r, b2i = e2
    ar = a2r * a1r - a2i * a1i
    ai = a2r * a1i + a2i * a1r
    br = a2r * b1r - a2i * b1i + b2r
    bi = a2r * b1i + a2i * b1r + b2i
    return (ar, ai, br, bi)

def s5_mixer(u, lam_re, lam_im, log_dt, b_re, b_im, c_re, c_im, d_skip, w_glu):
    bsz, s, _ = u.shape
    u32 = u.astype(F32).reshape(bsz, s, S5_G, S5_H)
    lam_re = lam_re.astype(F32)
    lam_im = lam_im.astype(F32)
    dt = jnp.exp(log_dt.astype(F32))[:, None]
    mag = jnp.exp(lam_re * dt)
    ang = lam_im * dt
    lb_re = mag * jnp.cos(ang)
    lb_im = mag * jnp.sin(ang)
    den = lam_re * lam_re + lam_im * lam_im
    num_re = lb_re - 1.0
    f_re = (num_re * lam_re + lb_im * lam_im) / den
    f_im = (lb_im * lam_re - num_re * lam_im) / den
    b_re = b_re.astype(F32)
    b_im = b_im.astype(F32)
    bb_re = f_re[..., None] * b_re - f_im[..., None] * b_im
    bb_im = f_re[..., None] * b_im + f_im[..., None] * b_re
    bu_re = jnp.einsum('bsgh,gph->sbgp', u32, bb_re)
    bu_im = jnp.einsum('bsgh,gph->sbgp', u32, bb_im)
    a_re = jnp.broadcast_to(lb_re[None, None], (s, 1, S5_G, S5_P))
    a_im = jnp.broadcast_to(lb_im[None, None], (s, 1, S5_G, S5_P))
    _, _, st_re, st_im = lax.associative_scan(
        _complex_linear_combine, (a_re, a_im, bu_re, bu_im), axis=0)
    y = (jnp.einsum('sbgp,ghp->bsgh', st_re, c_re.astype(F32))
         - jnp.einsum('sbgp,ghp->bsgh', st_im, c_im.astype(F32))
         + d_skip.astype(F32) * u32)
    y = jax.nn.gelu(y.reshape(bsz, s, D_A))
    out = y * jax.nn.sigmoid(y @ w_glu.astype(F32))
    return out.astype(u.dtype)

def pool_mixer(v, pool_w, pool_scale):
    bsz, s, _ = v.shape
    v32 = v.astype(F32).reshape(bsz, s, POOL_GROUPS, POOL_C)
    csum = jnp.cumsum(v32, axis=1)
    t = jnp.arange(s)
    means = []
    for gi, w in enumerate(POOL_WINDOWS):
        c = csum[:, :, gi]
        lagged = jnp.pad(c, ((0, 0), (w, 0), (0, 0)))[:, :s]
        count = jnp.minimum(t + 1, w).astype(F32)[None, :, None]
        means.append((c - lagged) / count)
    pooled = jnp.stack(means, axis=2) - v32
    mixed = jnp.einsum('bsgc,gcd->bsgd', pooled, pool_w.astype(F32))
    return (mixed.reshape(bsz, s, D_B) * pool_scale.astype(F32)).astype(v.dtype)

def stick_breaking_attention(qkv):
    bsz, s, _ = qkv.shape
    q, k, v = jnp.split(qkv.astype(F32), 3, axis=-1)
    to_heads = lambda z: z.reshape(bsz, s, SB_HEADS, SB_HEAD_DIM).transpose(0, 2, 1, 3)
    q, k, v = to_heads(q), to_heads(k), to_heads(v)
    scale = SB_HEAD_DIM ** -0.5
    outs = []
    for blk in range(s // SB_BLOCK):
        q0 = blk * SB_BLOCK
        end = q0 + SB_BLOCK
        z = jnp.einsum('bhqd,bhkd->bhqk', q[:, :, q0:end], k[:, :, :end]) * scale
        t_pos = q0 + jnp.arange(SB_BLOCK)
        s_pos = jnp.arange(end)
        causal = s_pos[None, :] < t_pos[:, None]
        log_keep = jnp.where(causal, jax.nn.log_sigmoid(-z), 0.0)
        log_after = lax.cumsum(log_keep, axis=3, reverse=True) - log_keep
        wts = jnp.where(causal, jnp.exp(jax.nn.log_sigmoid(z) + log_after), 0.0)
        outs.append(jnp.einsum('bhqk,bhkd->bhqd', wts, v[:, :, :end]))
    o = jnp.concatenate(outs, axis=2)
    return o.transpose(0, 2, 1, 3).reshape(bsz, s, D_MODEL).astype(qkv.dtype)

def grouped_moe(x, router_w, router_bias, w1, w3, w2):
    bsz, s, d = x.shape
    xt = x.reshape(-1, d)
    scores = jax.nn.sigmoid((xt @ router_w).astype(F32))
    sel = scores + router_bias.astype(F32)
    grp = sel.reshape(-1, N_EXPERT_GROUPS, EXPERTS_PER_GROUP)
    grp_score = jnp.sum(lax.top_k(grp, TOP_K)[0], axis=-1)
    top_group = jnp.argmax(grp_score, axis=-1)
    in_group = (jnp.arange(N_EXPERTS) // EXPERTS_PER_GROUP)[None, :] == top_group[:, None]
    _, idx = lax.top_k(jnp.where(in_group, sel, -jnp.inf), TOP_K)
    w = jnp.take_along_axis(scores, idx, axis=-1)
    w = w / jnp.sum(w, axis=-1, keepdims=True)
    gates = jnp.sum(jax.nn.one_hot(idx, N_EXPERTS, dtype=F32) * w[..., None], axis=1)
    h = jax.nn.silu(jnp.einsum('td,edf->etf', xt, w1)) * jnp.einsum('td,edf->etf', xt, w3)
    h = h * gates.T[:, :, None].astype(h.dtype)
    y = jnp.einsum('etf,efd->td', h, w2)
    return y.reshape(bsz, s, d).astype(x.dtype)

def first_inputs(seed: int = 0) -> dict:
    key = jax.random.key(seed)
    ks = jax.random.split(key, 32)
    nrm = lambda k, shape, sc: jax.random.normal(k, shape, F32) * sc
    n_idx = jnp.arange(S5_P, dtype=F32)
    return {
        'x': nrm(ks[0], (BATCH, SEQ, D_MODEL), 1.0),
        'p': nrm(ks[1], (DEPTH, BATCH, SEQ, PLE_DIM), 1.0),
        'ab_w_in': nrm(ks[2], (N_EVEN, D_MODEL, D_A + D_B), D_MODEL ** -0.5),
        's5_lambda_re': -0.5 + nrm(ks[3], (N_EVEN, S5_G, S5_P), 0.01),
        's5_lambda_im': math.pi * n_idx + nrm(ks[4], (N_EVEN, S5_G, S5_P), 0.01),
        's5_log_dt': jax.random.uniform(ks[5], (N_EVEN, S5_G), F32, math.log(DT_MIN), math.log(DT_MAX)),
        's5_b_re': nrm(ks[6], (N_EVEN, S5_G, S5_P, S5_H), (2 * S5_H) ** -0.5),
        's5_b_im': nrm(ks[7], (N_EVEN, S5_G, S5_P, S5_H), (2 * S5_H) ** -0.5),
        's5_c_re': nrm(ks[8], (N_EVEN, S5_G, S5_H, S5_P), S5_P ** -0.5),
        's5_c_im': nrm(ks[9], (N_EVEN, S5_G, S5_H, S5_P), S5_P ** -0.5),
        's5_d': nrm(ks[10], (N_EVEN, S5_G, S5_H), 1.0),
        's5_w_glu': nrm(ks[11], (N_EVEN, D_A, D_A), D_A ** -0.5),
        'pool_w': nrm(ks[12], (N_EVEN, POOL_GROUPS, POOL_C, POOL_C), POOL_C ** -0.5),
        'pool_scale': 1.0 + nrm(ks[13], (N_EVEN, D_B), 0.1),
        'ab_w_out': nrm(ks[14], (N_EVEN, D_A + D_B, D_MODEL), (D_A + D_B) ** -0.5 * DEEPNORM_BETA),
        'sb_w_qkv': nrm(ks[15], (N_ODD, D_MODEL, 3 * D_MODEL), D_MODEL ** -0.5),
        'sb_w_out': nrm(ks[16], (N_ODD, D_MODEL, D_MODEL), D_MODEL ** -0.5 * DEEPNORM_BETA),
        'ln_mix_g': 1.0 + nrm(ks[17], (DEPTH, D_MODEL), 0.01),
        'ln_mix_b': nrm(ks[18], (DEPTH, D_MODEL), 0.01),
        'ln_ffn_g': 1.0 + nrm(ks[19], (DEPTH, D_MODEL), 0.01),
        'ln_ffn_b': nrm(ks[20], (DEPTH, D_MODEL), 0.01),
        'router_w': nrm(ks[21], (D_MODEL, N_EXPERTS), D_MODEL ** -0.5),
        'router_bias': nrm(ks[22], (N_EXPERTS,), 0.01),
        'moe_w1': nrm(ks[23], (DEPTH, N_EXPERTS, D_MODEL, D_EXPERT), D_MODEL ** -0.5),
        'moe_w3': nrm(ks[24], (DEPTH, N_EXPERTS, D_MODEL, D_EXPERT), D_MODEL ** -0.5),
        'moe_w2': nrm(ks[25], (DEPTH, N_EXPERTS, D_EXPERT, D_MODEL), D_EXPERT ** -0.5 * DEEPNORM_BETA),
        'ple_w_proj': nrm(ks[26], (DEPTH, PLE_DIM, D_MODEL), PLE_DIM ** -0.5 * DEEPNORM_BETA),
        'ple_w_gate': nrm(ks[27], (DEPTH, D_MODEL, D_MODEL), D_MODEL ** -0.5),
    }

def first_block(x, p, ab_w_in, s5_lambda_re, s5_lambda_im, s5_log_dt, s5_b_re, s5_b_im,
              s5_c_re, s5_c_im, s5_d, s5_w_glu, pool_w, pool_scale, ab_w_out,
              sb_w_qkv, sb_w_out, ln_mix_g, ln_mix_b, ln_ffn_g, ln_ffn_b,
              router_w, router_bias, moe_w1, moe_w3, moe_w2, ple_w_proj, ple_w_gate):
    for i in range(DEPTH):
        j = i // 2
        if i % 2 == 0:
            h = x @ ab_w_in[j]
            out_a = s5_mixer(h[..., :D_A], s5_lambda_re[j], s5_lambda_im[j], s5_log_dt[j],
                             s5_b_re[j], s5_b_im[j], s5_c_re[j], s5_c_im[j], s5_d[j], s5_w_glu[j])
            out_b = pool_mixer(h[..., D_A:], pool_w[j], pool_scale[j])
            mix = jnp.concatenate([out_a, out_b], axis=-1) @ ab_w_out[j]
        else:
            mix = stick_breaking_attention(x @ sb_w_qkv[j]) @ sb_w_out[j]
        x = layer_norm(DEEPNORM_ALPHA * x + mix, ln_mix_g[i], ln_mix_b[i])
        ple = (p[i] @ ple_w_proj[i]) * jax.nn.sigmoid(x @ ple_w_gate[i])
        ffn = grouped_moe(x, router_w, router_bias, moe_w1[i], moe_w3[i], moe_w2[i])
        x = layer_norm(DEEPNORM_ALPHA * x + ffn + ple, ln_ffn_g[i], ln_ffn_b[i])
    return x


DEPTH_2 = 4

N_MIXERS = 3
N_CONV_LAYERS = (DEPTH_2 + 2) // 3
N_LRU_LAYERS = (DEPTH_2 + 1) // 3
N_MLA_LAYERS = DEPTH_2 // 3

CONV_WIDTH = 3

LRU_WIDTH = 1280
LRU_BLOCKS = 10
LRU_BLOCK_W = LRU_WIDTH // LRU_BLOCKS
LRU_CONV_WIDTH = 4
LRU_C = 8.0

MLA_HEADS = 8
Q_LORA_RANK = 384
KV_LORA_RANK = 256
QK_NOPE_DIM = 128
QK_ROPE_DIM = 64
V_HEAD_DIM = 128
ROPE_THETA = 10000.0
Q_BLOCK = 128

D_FF = ((8 * D_MODEL // 3 + 255) // 256) * 256

NORM_EPS = 1e-6


def rms_norm(x, g):
    xf = x.astype(jnp.float32)
    y = xf * lax.rsqrt(jnp.mean(xf * xf, axis=-1, keepdims=True) + NORM_EPS)
    return (y * g.astype(jnp.float32)).astype(x.dtype)

def causal_depthwise_conv(x, w):
    width, ch = w.shape
    return lax.conv_general_dilated(
        x, w[:, None, :].astype(x.dtype), window_strides=(1,),
        padding=[(width - 1, 0)], dimension_numbers=('NWC', 'WIO', 'NWC'),
        feature_group_count=ch)

def short_conv_mixer(xn, w_in, w_conv, w_out):
    b_gate, c_gate, h = jnp.split(xn @ w_in, 3, axis=-1)
    y = b_gate * causal_depthwise_conv(c_gate * h, w_conv)
    return y @ w_out

def rg_lru(xs, wa, ba, wx, bx, lam):
    bsz, seq, width = xs.shape
    xb = xs.reshape(bsz, seq, LRU_BLOCKS, LRU_BLOCK_W)
    r = jax.nn.sigmoid(jnp.einsum('bsnd,nde->bsne', xb, wa) + ba).reshape(bsz, seq, width)
    i = jax.nn.sigmoid(jnp.einsum('bsnd,nde->bsne', xb, wx) + bx).reshape(bsz, seq, width)
    log_a = LRU_C * r.astype(jnp.float32) * jax.nn.log_sigmoid(lam.astype(jnp.float32))
    a = jnp.exp(log_a)
    mult = jnp.sqrt(-jnp.expm1(2.0 * log_a))
    b = mult * (i * xs).astype(jnp.float32)

    def combine(left, right):
        a_l, b_l = left
        a_r, b_r = right
        return a_l * a_r, a_r * b_l + b_r

    _, h = lax.associative_scan(combine, (a, b), axis=1)
    return h.astype(xs.dtype)

def recurrent_mixer(xn, w_in, conv_w, conv_b, gate_a_w, gate_a_b, gate_x_w, gate_x_b, lam, w_out):
    gate_branch, rec_branch = jnp.split(xn @ w_in, 2, axis=-1)
    gate = jax.nn.gelu(gate_branch, approximate=True)
    rec = causal_depthwise_conv(rec_branch, conv_w) + conv_b
    h = rg_lru(rec, gate_a_w, gate_a_b, gate_x_w, gate_x_b, lam)
    return (gate * h) @ w_out

def apply_rope(t, cos, sin):
    half = t.shape[-1] // 2
    tf = t.astype(jnp.float32)
    t1, t2 = tf[..., :half], tf[..., half:]
    return jnp.concatenate([t1 * cos - t2 * sin, t2 * cos + t1 * sin], axis=-1).astype(t.dtype)

def mla_mixer(xn, cos, sin, w_down, q_norm, kv_norm, w_uq, w_ukv,
              qn_norm, qr_norm, kn_norm, kr_norm, w_o):
    bsz, seq, _ = xn.shape
    c = xn @ w_down
    c_q = c[..., :Q_LORA_RANK]
    c_kv = c[..., Q_LORA_RANK:Q_LORA_RANK + KV_LORA_RANK]
    k_rope = c[..., Q_LORA_RANK + KV_LORA_RANK:]

    q = (rms_norm(c_q, q_norm) @ w_uq).reshape(bsz, seq, MLA_HEADS, QK_NOPE_DIM + QK_ROPE_DIM)
    kv = (rms_norm(c_kv, kv_norm) @ w_ukv).reshape(bsz, seq, MLA_HEADS, QK_NOPE_DIM + V_HEAD_DIM)
    q_nope = rms_norm(q[..., :QK_NOPE_DIM], qn_norm)
    q_rope = apply_rope(rms_norm(q[..., QK_NOPE_DIM:], qr_norm), cos[:, :, None, :], sin[:, :, None, :])
    k_nope = rms_norm(kv[..., :QK_NOPE_DIM], kn_norm)
    v = kv[..., QK_NOPE_DIM:]
    k_rope = apply_rope(rms_norm(k_rope, kr_norm), cos, sin)

    scale = 1.0 / math.sqrt(QK_NOPE_DIM + QK_ROPE_DIM)
    n_blk = seq // Q_BLOCK

    def to_blocks(t):
        return t.reshape(bsz, n_blk, Q_BLOCK, *t.shape[2:]).transpose(1, 0, 2, 3, 4)

    k_idx = jnp.arange(seq)

    def attend(args):
        qn_b, qr_b, start = args
        s = (jnp.einsum('bqhd,bkhd->bhqk', qn_b, k_nope)
             + jnp.einsum('bqhr,bkr->bhqk', qr_b, k_rope)).astype(jnp.float32) * scale
        q_idx = start + jnp.arange(Q_BLOCK)
        mask = k_idx[None, :] <= q_idx[:, None]
        s = jnp.where(mask, s, jnp.finfo(jnp.float32).min)
        p = jax.nn.softmax(s, axis=-1).astype(v.dtype)
        return jnp.einsum('bhqk,bkhd->bqhd', p, v)

    starts = jnp.arange(n_blk, dtype=jnp.int32) * Q_BLOCK
    o = lax.map(attend, (to_blocks(q_nope), to_blocks(q_rope), starts))
    o = o.transpose(1, 0, 2, 3, 4).reshape(bsz, seq, MLA_HEADS * V_HEAD_DIM)
    return o @ w_o

def swiglu_ffn(xn, w_gu, w_down):
    gate, up = jnp.split(xn @ w_gu, 2, axis=-1)
    return (jax.nn.silu(gate) * up) @ w_down

def second_inputs(seed: int = 0) -> dict:
    key = jax.random.key(seed)
    ks = iter(jax.random.split(key, 40))
    f32 = jnp.float32
    res = (2 * DEPTH_2) ** -0.5

    def nrm(shape, scale):
        return jax.random.normal(next(ks), shape, f32) * scale

    def gain(shape):
        return 1.0 + 0.05 * jax.random.normal(next(ks), shape, f32)

    x = jax.random.normal(next(ks), (BATCH, SEQ, D_MODEL), f32)
    offset = jax.random.randint(next(ks), (BATCH, 1), 0, 1024, dtype=jnp.int32)
    positions = offset + jnp.arange(SEQ, dtype=jnp.int32)[None, :]

    mix_norm = gain((DEPTH_2, D_MODEL))

    nA = N_CONV_LAYERS
    conv_w_in = nrm((nA, D_MODEL, 3 * D_MODEL), D_MODEL ** -0.5)
    conv_w = nrm((nA, CONV_WIDTH, D_MODEL), CONV_WIDTH ** -0.5)
    conv_w_out = nrm((nA, D_MODEL, D_MODEL), D_MODEL ** -0.5 * res)

    nB = N_LRU_LAYERS
    lru_w_in = nrm((nB, D_MODEL, 2 * LRU_WIDTH), D_MODEL ** -0.5)
    lru_conv_w = nrm((nB, LRU_CONV_WIDTH, LRU_WIDTH), LRU_CONV_WIDTH ** -0.5)
    lru_conv_b = nrm((nB, LRU_WIDTH), 0.01)
    lru_gate_a_w = nrm((nB, LRU_BLOCKS, LRU_BLOCK_W, LRU_BLOCK_W), LRU_BLOCK_W ** -0.5)
    lru_gate_a_b = nrm((nB, LRU_BLOCKS, LRU_BLOCK_W), 0.01)
    lru_gate_x_w = nrm((nB, LRU_BLOCKS, LRU_BLOCK_W, LRU_BLOCK_W), LRU_BLOCK_W ** -0.5)
    lru_gate_x_b = nrm((nB, LRU_BLOCKS, LRU_BLOCK_W), 0.01)
    a0 = jax.random.uniform(next(ks), (nB, LRU_WIDTH), f32, 0.9, 0.999)
    lru_lambda = jnp.log(a0) - jnp.log1p(-a0)
    lru_w_out = nrm((nB, LRU_WIDTH, D_MODEL), LRU_WIDTH ** -0.5 * res)

    nC = N_MLA_LAYERS
    mla_w_down = nrm((nC, D_MODEL, Q_LORA_RANK + KV_LORA_RANK + QK_ROPE_DIM), D_MODEL ** -0.5)
    mla_q_norm = gain((nC, Q_LORA_RANK))
    mla_kv_norm = gain((nC, KV_LORA_RANK))
    mla_w_uq = nrm((nC, Q_LORA_RANK, MLA_HEADS * (QK_NOPE_DIM + QK_ROPE_DIM)), Q_LORA_RANK ** -0.5)
    mla_w_ukv = nrm((nC, KV_LORA_RANK, MLA_HEADS * (QK_NOPE_DIM + V_HEAD_DIM)), KV_LORA_RANK ** -0.5)
    mla_qn_norm = gain((nC, QK_NOPE_DIM))
    mla_qr_norm = gain((nC, QK_ROPE_DIM))
    mla_kn_norm = gain((nC, QK_NOPE_DIM))
    mla_kr_norm = gain((nC, QK_ROPE_DIM))
    mla_w_o = nrm((nC, MLA_HEADS * V_HEAD_DIM, D_MODEL), (MLA_HEADS * V_HEAD_DIM) ** -0.5 * res)

    ffn_norm = gain((DEPTH_2, D_MODEL))
    ffn_w_gu = nrm((DEPTH_2, D_MODEL, 2 * D_FF), D_MODEL ** -0.5)
    ffn_w_down = nrm((DEPTH_2, D_FF, D_MODEL), D_FF ** -0.5 * res)

    return {'x': x, 'positions': positions, 'mix_norm': mix_norm,
            'conv_w_in': conv_w_in, 'conv_w': conv_w, 'conv_w_out': conv_w_out,
            'lru_w_in': lru_w_in, 'lru_conv_w': lru_conv_w, 'lru_conv_b': lru_conv_b,
            'lru_gate_a_w': lru_gate_a_w, 'lru_gate_a_b': lru_gate_a_b,
            'lru_gate_x_w': lru_gate_x_w, 'lru_gate_x_b': lru_gate_x_b,
            'lru_lambda': lru_lambda, 'lru_w_out': lru_w_out,
            'mla_w_down': mla_w_down, 'mla_q_norm': mla_q_norm, 'mla_kv_norm': mla_kv_norm,
            'mla_w_uq': mla_w_uq, 'mla_w_ukv': mla_w_ukv,
            'mla_qn_norm': mla_qn_norm, 'mla_qr_norm': mla_qr_norm,
            'mla_kn_norm': mla_kn_norm, 'mla_kr_norm': mla_kr_norm, 'mla_w_o': mla_w_o,
            'ffn_norm': ffn_norm, 'ffn_w_gu': ffn_w_gu, 'ffn_w_down': ffn_w_down}

def second_block(x, positions, mix_norm, conv_w_in, conv_w, conv_w_out,
              lru_w_in, lru_conv_w, lru_conv_b, lru_gate_a_w, lru_gate_a_b,
              lru_gate_x_w, lru_gate_x_b, lru_lambda, lru_w_out,
              mla_w_down, mla_q_norm, mla_kv_norm, mla_w_uq, mla_w_ukv,
              mla_qn_norm, mla_qr_norm, mla_kn_norm, mla_kr_norm, mla_w_o,
              ffn_norm, ffn_w_gu, ffn_w_down):
    inv_freq = ROPE_THETA ** (-jnp.arange(0, QK_ROPE_DIM, 2, dtype=jnp.float32) / QK_ROPE_DIM)
    angle = positions.astype(jnp.float32)[..., None] * inv_freq
    cos, sin = jnp.cos(angle), jnp.sin(angle)

    h = x
    for i in range(DEPTH_2):
        kind, j = i % N_MIXERS, i // N_MIXERS
        xn = rms_norm(h, mix_norm[i])
        if kind == 0:
            y = short_conv_mixer(xn, conv_w_in[j], conv_w[j], conv_w_out[j])
        elif kind == 1:
            y = recurrent_mixer(xn, lru_w_in[j], lru_conv_w[j], lru_conv_b[j],
                                lru_gate_a_w[j], lru_gate_a_b[j], lru_gate_x_w[j],
                                lru_gate_x_b[j], lru_lambda[j], lru_w_out[j])
        else:
            y = mla_mixer(xn, cos, sin, mla_w_down[j], mla_q_norm[j], mla_kv_norm[j],
                          mla_w_uq[j], mla_w_ukv[j], mla_qn_norm[j], mla_qr_norm[j],
                          mla_kn_norm[j], mla_kr_norm[j], mla_w_o[j])
        h = h + y
        h = h + swiglu_ffn(rms_norm(h, ffn_norm[i]), ffn_w_gu[i], ffn_w_down[i])
    return h


def setup_inputs(seed=0):
    out = dict(first_inputs(seed))
    for name, value in second_inputs(seed + 1).items():
        if name != "x":
            out[name + "_2"] = value
    return out


def reference(
    x, p, ab_w_in, s5_lambda_re, s5_lambda_im, s5_log_dt, s5_b_re, s5_b_im, s5_c_re, s5_c_im,
    s5_d, s5_w_glu, pool_w, pool_scale, ab_w_out, sb_w_qkv, sb_w_out, ln_mix_g, ln_mix_b,
    ln_ffn_g, ln_ffn_b, router_w, router_bias, moe_w1, moe_w3, moe_w2, ple_w_proj, ple_w_gate,
    positions_2, mix_norm_2, conv_w_in_2, conv_w_2, conv_w_out_2, lru_w_in_2, lru_conv_w_2,
    lru_conv_b_2, lru_gate_a_w_2, lru_gate_a_b_2, lru_gate_x_w_2, lru_gate_x_b_2, lru_lambda_2,
    lru_w_out_2, mla_w_down_2, mla_q_norm_2, mla_kv_norm_2, mla_w_uq_2, mla_w_ukv_2,
    mla_qn_norm_2, mla_qr_norm_2, mla_kn_norm_2, mla_kr_norm_2, mla_w_o_2, ffn_norm_2,
    ffn_w_gu_2, ffn_w_down_2,
):
    x = first_block(
        x, p, ab_w_in, s5_lambda_re, s5_lambda_im, s5_log_dt, s5_b_re, s5_b_im, s5_c_re,
        s5_c_im, s5_d, s5_w_glu, pool_w, pool_scale, ab_w_out, sb_w_qkv, sb_w_out, ln_mix_g,
        ln_mix_b, ln_ffn_g, ln_ffn_b, router_w, router_bias, moe_w1, moe_w3, moe_w2, ple_w_proj,
        ple_w_gate,
    )
    return second_block(
        x, positions_2, mix_norm_2, conv_w_in_2, conv_w_2, conv_w_out_2, lru_w_in_2,
        lru_conv_w_2, lru_conv_b_2, lru_gate_a_w_2, lru_gate_a_b_2, lru_gate_x_w_2,
        lru_gate_x_b_2, lru_lambda_2, lru_w_out_2, mla_w_down_2, mla_q_norm_2, mla_kv_norm_2,
        mla_w_uq_2, mla_w_ukv_2, mla_qn_norm_2, mla_qr_norm_2, mla_kn_norm_2, mla_kr_norm_2,
        mla_w_o_2, ffn_norm_2, ffn_w_gu_2, ffn_w_down_2,
    )


_drawn_inputs = setup_inputs


def setup_inputs(seed=0):
    import zlib

    import numpy as np

    out = dict(_drawn_inputs(seed))
    spreads = {}
    factors = {'s5_lambda_re': 8.0,
     's5_c_im': 2.755,
     'lru_conv_b_2': 8.0,
     'lru_gate_a_b_2': 8.0,
     'lru_gate_x_b_2': 8.0,
     'mla_q_norm_2': 8.0,
     'mla_kv_norm_2': 8.0,
     'mla_qn_norm_2': 8.0,
     'mla_qr_norm_2': 8.0,
     'mla_kn_norm_2': 8.0,
     'mla_kr_norm_2': 8.0}
    for name, (base, spread) in spreads.items():
        noise = np.random.default_rng([zlib.crc32(name.encode()), seed]).standard_normal(out[name].shape)
        drawn = base * np.exp(spread * noise) if base else spread * noise
        out[name] = jnp.asarray(drawn.astype(out[name].dtype))
    for name, factor in factors.items():
        out[name] = (out[name] * factor).astype(out[name].dtype)
    return out
```

```python
import math

import concourse.bass as bass
import numpy as np
from concourse import mybir
from contextlib import ExitStack

F32 = mybir.dt.float32
F32R = mybir.dt.float32r
BF16 = mybir.dt.bfloat16
I32 = mybir.dt.int32
ACT = mybir.ActivationFunctionType
ALU = mybir.AluOpType
AX = mybir.AxisListType

D = 1024
T = 256
P = 128
KC = D // P
BLOCKS_PER_TILE = 16
TILE = BLOCKS_PER_TILE * P
RING = 3
N_EXPERTS = 16
D_EXPERT = 512
D_FF = 2816
UNIT = 2 * P
ALPHA = 4.0 ** 0.25
LN_EPS = 1e-5
NORM_EPS = 1e-6
LRU_CHUNKS = 10
SCRATCH = 13312
NEG = 1e30
TWO_PI = 2.0 * math.pi
ROUND = 12582912.0

STAGES = [("s5",), ("moe", 0), ("sb",), ("moe", 1), ("conv", 0), ("ffn", 0), ("lru",), ("ffn", 1),
          ("mla",), ("ffn", 2), ("conv", 1), ("ffn", 3)]
LN_STAGES = ("s5", "moe", "sb")


def stage_blocks(stage):
    kind = stage[0]
    if kind == "s5":
        return 8 * 8 + 4 + 4 * 4 + 8 * 8
    if kind == "moe":
        return 2 * 8 + 8 * 8 + 3 * 16 * (N_EXPERTS * D_EXPERT // UNIT)
    if kind == "sb":
        return 8 * 24 + 8 * 8
    if kind == "conv":
        return 8 * 24 + 8 * 8
    if kind == "lru":
        return 8 * 20 + 20 + 10 * 8
    if kind == "mla":
        return 8 * 7 + 3 * 12 + 2 * 16 + 8 * 8
    return 3 * 16 * (D_FF // UNIT)


def stream_plan(stages):
    starts, at = [], 0
    for stage in stages:
        starts.append(at)
        at += -(-stage_blocks(stage) // BLOCKS_PER_TILE)
    return starts, -(-(at + 2) // RING) * RING


SIGNALS = {
    "pe": ["tile", "y", "sum", "sum of squares",
           "h1", "h3", "ple", "logits", "ple gate", "gates",
           "uv", "drive", "pooled", "read out", "glu",
           "qk", "v", "scores", "log weights", "values",
           "conv c", "conv h", "conv b", "rec", "gate", "r", "i",
           "down", "latent sums", "raw", "raw2", "pair sums", "mla v", "turned"],
    "act": ["step", "p_hi", "x_hi", "x squared", "rms seed", "sq", "seed", "c_hi",
            "h1 read", "silu", "h_hi", "router tanh", "ple tanh", "gate copy",
            "dt", "mag", "sine", "uv", "pooled hi", "yg hi", "glu",
            "q", "log", "weights",
            "lam", "inner hi", "r", "i", "a", "root", "gelu",
            "latent squared", "latent seed", "latent hi", "rotation", "squared pair", "pair seed", "exp", "turned copy"],
    "dve": ["step", "p_lo", "x", "x times gain", "x_lo", "rms variance", "z", "centred", "variance", "normed", "c_lo",
            "h1 read", "gated", "h", "h_lo", "gates", "ple part",
            "log mag", "theta", "minus c_im", "rotated", "r", "scanned", "states", "pooled", "pooled lo", "pool out",
            "s5 y", "yg lo", "gated y",
            "k", "v copy", "softplus", "conv c", "conv h", "conv b", "conv out",
            "rec", "convolved", "inner lo", "gate", "half bias", "log a", "minus b2",
            "latent", "latent variance", "latent normed", "latent lo", "angle", "pair variance", "normed pair", "rope",
            "mla v copy", "minus max", "probabilities"],
    "pool": ["step", "ones", "zeros", "window sums", "states"],
}


class Did:

    def __init__(self, semaphores, known):
        self.semaphores, self.known = semaphores, known
        self.new, self.count, self.last, self.turn = {}, {}, None, None

    def __getitem__(self, name):
        return self.semaphores[name]

    def next(self, name, *index, tile=None):
        self.last = name
        self.count[name] = self.count.get(name, 0) + 1
        if self.turn is None:
            self.note(name, index, tile, self.count[name])
        else:
            self.turn.append((name, index, tile, self.count[name]))
        return 1

    def note(self, name, index, tile, count):
        self.new[(name,) + index] = count
        if tile is not None:
            self.new["tile", tile] = (name, count)

    def begin_loop(self):
        self.turn, self.before = [], dict(self.count)

    def end_loop(self, turns):
        step = {name: n - self.before.get(name, 0) for name, n in self.count.items()}
        for name, index, tile, count in self.turn:
            for i in range(turns):
                self.note(name, index[:-1] + (index[-1] + 2 * i,) if index else index,
                          None if tile is None else tile + 6 * i, count + i * step[name])
        for name in self.count:
            self.count[name] += (turns - 1) * step[name]
        self.turn = None

    def at(self, name, *index, turn=None, turns=None):
        if not self.known:
            return 1
        if turn is None:
            return self.known[(name,) + index]
        counts = [self.known[(name,) + index[:-1] + (index[-1] + 2 * i,)] for i in range(turns)]
        return self.evenly(counts, turn)

    def tile(self, n, turn=None, turns=1):
        if not self.known:
            return self.semaphores["tile"], 1
        at = [self.known["tile", n + 6 * i] for i in range(turns)]
        assert all(name == at[0][0] for name, _ in at)
        counts = [count for _, count in at]
        return self.semaphores[at[0][0]], counts[0] if turn is None else self.evenly(counts, turn)

    def evenly(self, counts, turn):
        step = counts[1] - counts[0]
        assert all(b - a == step for a, b in zip(counts, counts[1:])), counts
        return turn * step + counts[0]


def build(nc, dram, columns, stages, known):
    starts, n_tiles = stream_plan(stages)
    ctx = ExitStack()
    with ctx:
        def sb(name, shape, dtype=F32):
            return ctx.enter_context(nc.sbuf_tensor(name, shape, dtype))

        def sem(name):
            return ctx.enter_context(nc.semaphore(name))

        raw = sb("raw", [P, RING, TILE])
        w_hi = sb("w_hi", [P, RING, TILE], F32R)
        w_lo = sb("w_lo", [P, RING, TILE], F32R)
        x = sb("x", [P, KC, T])
        x_hi = sb("x_hi", [P, KC, T], F32R)
        x_lo = sb("x_lo", [P, KC, T], F32R)
        c_hi = sb("c_hi", [P, LRU_CHUNKS, T], F32R)
        c_lo = sb("c_lo", [P, LRU_CHUNKS, T], F32R)
        p_hi = sb("p_hi", [P, 4, T], F32R)
        p_lo = sb("p_lo", [P, 4, T], F32R)
        scr = sb("scr", [P, SCRATCH])
        hidden_buf = sb("hidden_buf", [P, 8, T])
        h1n, silu_h, gated, h = (hidden_buf[:, 2 * i:2 * i + 2, :] for i in range(4))
        h_hi = sb("h_hi", [P, 2, T], F32R)
        h_lo = sb("h_lo", [P, 2, T], F32R)
        rstd = sb("rstd", [P, T])
        var = sb("var", [P, T])
        tmp_r = sb("tmp_r", [P, T])
        tmp_n = sb("tmp_n", [P, T])
        par = sb("par", [P, columns["total"]])
        small = sb("small", [P, 128])
        positions = sb("positions", [P, T], I32)
        ones = sb("ones", [P, P])
        zeros = sb("zeros", [P, 2 * T], BF16)
        psum = [ctx.enter_context(nc.psum_tensor(f"bank{i}", [P, 2 * T], F32)) for i in range(8)]
        Q, Y = psum[:4], psum[4:]

        raw_in = [sem(f"raw_in{i}") for i in range(RING)]
        hi_done = sem("hi_done")
        lo_done = sem("lo_done")
        x_in = sem("x_in")
        par_in = sem("par_in")
        p_in = sem("p_in")
        pos_in = sem("pos_in")
        s5_in = sem("s5_in")
        s5_par_in = sem("s5_par_in")
        out_done = sem("out_done")
        did = {who: Did({name: sem(f"{who}_{name.replace(' ', '_')}") for name in names},
                        known and known[who]) for who, names in SIGNALS.items()}
        pe_did, act_did, dve_did, pool_did = did["pe"], did["act"], did["dve"], did["pool"]

        def region(at, *shape):
            size = math.prod(shape)
            ap = scr[:, at:at + size]
            if len(shape) == 2:
                return ap.rearrange("p (a b) -> p a b", b=shape[1])
            if len(shape) == 3:
                return ap.rearrange("p (a b c) -> p a b c", b=shape[1], c=shape[2])
            return ap

        def column(name, i=0, n=1):
            at = columns[name] + i
            return par[:, at:at + n]

        def pair(ap, i):
            return ap[:, 2 * i:2 * i + 2, :]

        def bank(b):
            return b[:, :].rearrange("p (a t) -> p a t", t=T)

        def over_pair(ap):
            return ap.unsqueeze(1).to_broadcast([P, 2, T])

        def over_tokens(ap, n=2):
            return ap.unsqueeze(2).to_broadcast([P, n, T])

        z = region(9216, KC, T)
        squares = region(11264, KC, T)
        gates = region(0, N_EXPERTS, T)
        x_alpha = region(4096, KC, T)
        ple_tanh = region(6144, KC, T)
        ple_part = region(8192, 2, T)
        routing = region(8704, 512)

        class Stream:
            def __init__(self):
                self.tile = 0
                self.block = 0
        act_at, dve_at, pe_at = Stream(), Stream(), Stream()

        def split_hi(act, i=None, times=0, n=None):
            if i is None:
                n = act_at.tile
                act_at.tile += 1
                act.wait_ge(raw_in[n % RING], 16 * (n // RING + 1))
                if n >= RING:
                    used, count = pe_did.tile(n - RING)
                    act.wait_ge(used, count)
            else:
                act.wait_ge(raw_in[n % RING], i * 32 + 16 * (n // RING + 1))
                used, count = pe_did.tile(n - RING, turn=i, turns=times)
                act.wait_ge(used, count)
            nc.scalar.activation(w_hi[:, n % RING, :], raw[:, n % RING, :], ACT.Copy).then_inc(hi_done, 1)

        def split_lo(dve, i=None, n=None):
            if i is None:
                n = dve_at.tile
                dve_at.tile += 1
                dve.wait_ge(hi_done, n + 1)
            else:
                dve.wait_ge(hi_done, i * 6 + n + 1)
            nc.vector.tensor_tensor(w_lo[:, n % RING, :], raw[:, n % RING, :],
                                    w_hi[:, n % RING, :].bitcast(F32), ALU.subtract).then_inc(lo_done, 1)

        def block_of(t, b):
            s = slice(b * P, (b + 1) * P)
            return w_hi[:, t % RING, s], w_lo[:, t % RING, s]

        def three(out, hi, lo, xh, xl, start, stop, shared=False):
            nc.tensor.matmul(out, hi, xh, start=start, stop=False, skip_group_check=shared)
            nc.tensor.matmul(out, hi, xl, start=False, stop=False, skip_group_check=shared)
            return nc.tensor.matmul(out, lo, xh, start=False, stop=stop, skip_group_check=shared)

        def next_block(pe):
            t, b = divmod(pe_at.block, BLOCKS_PER_TILE)
            if b == 0:
                pe.wait_ge(lo_done, t + 1)
            pe_at.block += 1
            return t, b

        def signal_product(last, result, t, b):
            tile = t if b == BLOCKS_PER_TILE - 1 else None
            if result:
                last.then_inc(pe_did[result[0]], pe_did.next(*result, tile=tile))
            elif tile is not None:
                last.then_inc(pe_did["tile"], pe_did.next("tile", tile=tile))

        def product(pe, n_out, ks, xh, xl, out, fill, ready=None, add=(True, True)):
            for n in range(n_out):
                for k in range(ks):
                    if n == 0 and ready is not None:
                        ready(k)
                    t, b = next_block(pe)
                    hi, lo = block_of(t, b)
                    if k == 0 and n % 2 == 0:
                        before(pe, out(n)[0])
                    last = three(out(n)[1], hi, lo, xh[:, k, :], xl[:, k, :], add[0] and k == 0, add[1] and k == ks - 1,
                                 shared=add != (True, True))
                    signal_product(last, fill(n) if k == ks - 1 else None, t, b)

        def end_stream_stage(pe, st):
            t, b = divmod(pe_at.block, BLOCKS_PER_TILE)
            if b:
                nc.tensor.matmul(Q[2][:, 0:P], zeros[:, 0:P], zeros[:, 0:P], start=True, stop=True).then_inc(
                    pe_did["tile"], pe_did.next("tile", tile=t))
                pe_at.block = (t + 1) * BLOCKS_PER_TILE
            assert pe_at.block == BLOCKS_PER_TILE * (starts + [n_tiles])[st + 1] or st + 1 == len(stages)

        drained = {}

        def number(b):
            return next(i for i, other in enumerate(psum) if other is b)

        def before(pe, b):
            for who, label in drained.pop(number(b), []):
                pe.wait_ge(did[who][label[0]], did[who].at(*label))

        def after(b, *readers):
            drained[number(b)] = list(readers)

        def kind(st):
            return "raw" if st < len(stages) and stages[st][0] in LN_STAGES else ("rms" if st < len(stages) else "end")

        def gain(st):
            s = stages[st]
            name = "ffn_norm" if s[0] == "ffn" else "mix_norm"
            i = s[1] if s[0] == "ffn" else {"conv0": 0, "lru": 1, "mla": 2, "conv1": 3}[s[0] + "".join(map(str, s[1:]))]
            return name, 8 * i

        def ln_gain(st):
            s = stages[st]
            if s[0] == "moe":
                return "ln_ffn_g", "ln_ffn_b", 8 * s[1]
            return "ln_mix_g", "ln_mix_b", 8 * (s[0] == "sb")

        def link(engine, who, ins):
            ins.then_inc(did[who]["step"], did[who].next("step"))
            engine.wait_ge(did[who]["step"], did[who].count["step"])

        def settle(engine, who):
            if did[who].last:
                engine.wait_ge(did[who][did[who].last], did[who].count[did[who].last])

        def rsqrt_act(act, v, r, label):
            link(act, "act", nc.scalar.activation(r, v, ACT.Ln))
            nc.scalar.activation(r, r, ACT.Exp, scale=-0.5).then_inc(act_did[label[0]], act_did.next(*label))

        def newton_dve(dve, v, r, scratch):
            link(dve, "dve", nc.vector.tensor_tensor(scratch, r, r, ALU.mult))
            link(dve, "dve", nc.vector.scalar_tensor_tensor(scratch, scratch, -0.5, v, ALU.mult, ALU.mult))
            link(dve, "dve", nc.vector.scalar_tensor_tensor(r, scratch, 1.5, r, ALU.add, ALU.mult))

        def close_pe(pe, st):
            if stages[st][0] in LN_STAGES:
                for src, name, b, out in ((z, "z", Q[0], "sum"), (squares, "sq", Q[1], "sum of squares")):
                    before(pe, b)
                    for i in range(4):
                        pe.wait_ge(did["dve" if name == "z" else "act"][name], did["dve" if name == "z" else "act"].at(name, st, i))
                        for k in (2 * i, 2 * i + 1):
                            last = nc.tensor.matmul(b[:, 0:T], ones[:, :], src[:, k, :], start=(k == 0), stop=(k == KC - 1))
                    last.then_inc(pe_did[out], pe_did.next(out, st))
                after(Q[0], ("dve", ("centred", st, 3)))
                after(Q[1], ("dve", ("variance", st)))

        def close_act(act, st):
            if stages[st][0] in LN_STAGES:
                nc.scalar.preload_act_table_set("natural_log_exp_and_others")
                for i in range(4):
                    act.wait_ge(dve_did["centred"], dve_did.at("centred", st, i))
                    nc.scalar.activation(pair(squares, i), pair(z, i), ACT.Square).then_inc(
                        act_did["sq"], act_did.next("sq", st, i))
                act.wait_ge(dve_did["variance"], dve_did.at("variance", st))
                rsqrt_act(act, var[:, :], tmp_r[:, :], ("seed", st))
            feed_act(act, st)

        def feed_act(act, st):
            nxt = kind(st + 1)
            if nxt == "end":
                return
            for i in range(4):
                if nxt == "raw":
                    if st >= 0:
                        act.wait_ge(dve_did["x"], dve_did.at("x", st, i))
                    nc.scalar.activation(pair(x_hi, i), pair(x, i), ACT.Copy).then_inc(
                        act_did["x_hi"], act_did.next("x_hi", st, i))
                else:
                    act.wait_ge(dve_did["x times gain"], dve_did.at("x times gain", st, i))
                    nc.scalar.activation(pair(x_hi, i), pair(z, i), ACT.Copy).then_inc(
                        act_did["x_hi"], act_did.next("x_hi", st, i))
                    nc.scalar.activation(pair(squares, i), pair(x, i), ACT.Square).then_inc(
                        act_did["x squared"], act_did.next("x squared", st, i))

        def close_dve(dve, st):
            layer_norm = stages[st][0] in LN_STAGES
            if layer_norm:
                for i in range(4):
                    dve.wait_ge(pe_did["y"], pe_did.at("y", st, i))
                    if stages[st][0] == "moe":
                        ins = nc.vector.tensor_tensor(pair(z, i), pair(x_alpha, i), bank(Y[i]), ALU.add)
                    else:
                        ins = nc.vector.scalar_tensor_tensor(pair(z, i), pair(x, i), ALPHA, bank(Y[i]), ALU.mult, ALU.add)
                    ins.then_inc(dve_did["z"], dve_did.next("z", st, i))
                dve.wait_ge(pe_did["sum"], pe_did.at("sum", st))
                for i in range(4):
                    mean = over_pair(Q[0][:, 0:T])
                    nc.vector.scalar_tensor_tensor(pair(z, i), mean, -1.0 / D, pair(z, i), ALU.mult, ALU.add).then_inc(
                        dve_did["centred"], dve_did.next("centred", st, i))
                dve.wait_ge(pe_did["sum of squares"], pe_did.at("sum of squares", st))
                nc.vector.tensor_scalar(var[:, :], Q[1][:, 0:T], 1.0 / D, LN_EPS, ALU.mult, ALU.add).then_inc(
                    dve_did["variance"], dve_did.next("variance", st))
                dve.wait_ge(act_did["seed"], act_did.at("seed", st))
                newton_dve(dve, var[:, :], tmp_r[:, :], tmp_n[:, :])
                g, b, at = ln_gain(st)
                for i in range(4):
                    nc.vector.tensor_tensor(pair(z, i), pair(z, i), over_pair(tmp_r[:, :]), ALU.mult).then_inc(
                        dve_did["normed"], dve_did.next("normed", st, i))
                    dve.wait_ge(dve_did["normed"], dve_did.at("normed", st, i))
                    for k in (2 * i, 2 * i + 1):
                        last = nc.vector.tensor_scalar(x[:, k, :], z[:, k, :], column(g, at + k), column(b, at + k), ALU.mult, ALU.add)
                    last.then_inc(dve_did["x"], dve_did.next("x", st, i))
                    feed_dve(dve, st, i)
            else:
                for i in range(4):
                    dve.wait_ge(pe_did["y"], pe_did.at("y", st, i))
                    nc.vector.tensor_tensor(pair(x, i), pair(x, i), bank(Y[i]), ALU.add).then_inc(
                        dve_did["x"], dve_did.next("x", st, i))
                    feed_dve(dve, st, i)
            feed_dve(dve, st, 4)

        def feed_dve(dve, st, i):
            nxt = kind(st + 1)
            if nxt == "end":
                return
            if i < 4 and nxt == "rms":
                name, at = gain(st + 1)
                if st >= 0:
                    dve.wait_ge(dve_did["x"], dve_did.at("x", st, i))
                nc.vector.tensor_tensor(pair(z, i), pair(x, i), over_tokens(column(name, at + 2 * i, 2)), ALU.mult).then_inc(
                    dve_did["x times gain"], dve_did.next("x times gain", st, i))
            if i > 0:
                j = i - 1
                src = z if nxt == "rms" else x
                dve.wait_ge(act_did["x_hi"], act_did.at("x_hi", st, j))
                nc.vector.tensor_tensor(pair(x_lo, j), pair(src, j), pair(x_hi, j).bitcast(F32), ALU.subtract).then_inc(
                    dve_did["x_lo"], dve_did.next("x_lo", st, j))

        def keep_warm(pe, n):
            before(pe, Q[2])
            for _ in range(n):
                nc.tensor.matmul(Q[2][:, 0:T], zeros[:, 0:P], zeros[:, 0:T], start=True, stop=True)

        def input_ready(pe, st):
            def ready(k):
                if k % 2 == 0:
                    keep_warm(pe, 5 if k else 20)
                    pe.wait_ge(dve_did["x_lo"], dve_did.at("x_lo", st - 1, k // 2))
            return ready

        def rms_pe(pe, st, b):
            before(pe, b)
            for i in range(4):
                pe.wait_ge(act_did["x squared"], act_did.at("x squared", st - 1, i))
                for k in (2 * i, 2 * i + 1):
                    last = nc.tensor.matmul(b[:, 0:T], ones[:, :], squares[:, k, :], start=(k == 0), stop=(k == KC - 1))
            last.then_inc(pe_did["sum of squares"], pe_did.next("sum of squares", st, "in"))
            after(b, ("dve", ("rms variance", st)))

        def rms_act(act, st):
            nc.scalar.preload_act_table_set("natural_log_exp_and_others")
            act.wait_ge(dve_did["rms variance"], dve_did.at("rms variance", st))
            rsqrt_act(act, var[:, :], rstd[:, :], ("rms seed", st))

        def rms_dve(dve, st, b):
            dve.wait_ge(pe_did["sum of squares"], pe_did.at("sum of squares", st, "in"))
            nc.vector.tensor_scalar(var[:, :], b[:, 0:T], 1.0 / D, NORM_EPS, ALU.mult, ALU.add).then_inc(
                dve_did["rms variance"], dve_did.next("rms variance", st))
            dve.wait_ge(act_did["rms seed"], act_did.at("rms seed", st))
            newton_dve(dve, var[:, :], rstd[:, :], tmp_n[:, :])

        def ffn_sizes(st):
            moe = stages[st][0] == "moe"
            units = N_EXPERTS * D_EXPERT // UNIT if moe else D_FF // UNIT
            first = starts[st] + (5 if moe else 0)
            return moe, units, (units - 1) // 2, (units - 1) % 2, first

        def up_tile(first, u):
            return first if u == 0 else first + 2 + 3 * (u - 1)

        def down_tile(first, units, u):
            return first + 4 + 3 * u if u < units - 1 else first + 2 + 3 * (units - 1)

        def ffn_pe(pe, st):
            moe, units, turns, extra, first = ffn_sizes(st)
            pe_at.block = first * BLOCKS_PER_TILE

            def wait_tile(n, i):
                if i is None:
                    pe.wait_ge(lo_done, n + 1)
                else:
                    pe.wait_ge(lo_done, i * 6 + n + 1)

            def up(u, i=None):
                t = up_tile(first, u)
                for which, b, name in ((0, Q[0], "h1"), (1, Q[1], "h3")):
                    wait_tile(t + which, i)
                    reader = ("h1 read", "h")[which]
                    who = "dve" if which or not moe else "act"
                    if u:
                        pe.wait_ge(did[who][reader], did[who].at(reader, st, u - 1, turn=i, turns=turns))
                    else:
                        before(pe, b)
                    for n in range(2):
                        for k in range(KC):
                            if u == 0 and which == 0 and n == 0 and i is None and not moe:
                                input_ready(pe, st)(k)
                            hi, lo = block_of(t + which, n * KC + k)
                            last = three(b[:, n * T:(n + 1) * T], hi, lo, x_hi[:, k, :], x_lo[:, k, :], k == 0, k == KC - 1)
                    last.then_inc(pe_did[name], pe_did.next(name, st, u, tile=t + which if u or which == 0 else None))
                    if u == 0 and which == 0 and i is None and not moe:
                        rms_pe(pe, st, Q[3])

            def down(u, i=None):
                t = down_tile(first, units, u)
                wait_tile(t, i)
                pe.wait_ge(dve_did["h_lo"], dve_did.at("h_lo", st, u, turn=i, turns=turns))
                final = i is None and u == units - 1
                for n in range(KC):
                    for f in range(2):
                        hi, lo = block_of(t, 2 * n + f)
                        last = three(Y[n // 2][:, n % 2 * T:(n % 2 + 1) * T], hi, lo, h_hi[:, f, :], h_lo[:, f, :],
                                     False, final and f == 1, shared=True)
                    if final and n % 2:
                        last.then_inc(pe_did["y"], pe_did.next("y", st, n // 2, tile=t if n == KC - 1 else None))
                if not final:
                    last.then_inc(pe_did["tile"], pe_did.next("tile", tile=t))

            up(0)
            for b in Y:
                before(pe, b)
                last = nc.tensor.matmul(b[:, :], zeros[:, 0:P], zeros[:, :], start=True, stop=False, skip_group_check=True)
                if b is Y[0]:
                    last.then_inc(pe_did["tile"], pe_did.next("tile", tile=first + 1))
            pe_did.begin_loop()
            with pe.Fori(0, turns) as i:
                up(1, i)
                down(0, i)
                up(2, i)
                down(1, i)
            pe_did.end_loop(turns)
            if extra:
                up(units - 1)
                down(units - 2)
            down(units - 1)
            after(Q[0], ("act" if moe else "dve", ("h1 read", st, units - 1)))
            after(Q[1], ("dve", ("h", st, units - 1)))
            for i in range(4):
                after(Y[i], ("dve", ("z" if moe else "x", st, i)))
            pe_at.block = (down_tile(first, units, units - 1) + 1) * BLOCKS_PER_TILE

        def ffn_act(act, st):
            moe, units, turns, extra, first = ffn_sizes(st)

            def hi(n, i):
                if i is None:
                    assert n == act_at.tile, (n, act_at.tile)
                    split_hi(act)
                else:
                    split_hi(act, i, turns, n)

            def silu(u, i=None):
                if moe:
                    act.wait_ge(pe_did["h1"], pe_did.at("h1", st, u, turn=i, turns=turns))
                    if i is not None or u:
                        act.wait_ge(dve_did["gated"], dve_did.at("gated", st, u - 1, turn=i, turns=turns))
                    nc.scalar.activation(silu_h[:, :, :], bank(Q[0]), ACT.Silu).then_inc(
                        act_did["h1 read"], act_did.next("h1 read", st, u))
                else:
                    act.wait_ge(dve_did["h1 read"], dve_did.at("h1 read", st, u, turn=i, turns=turns))
                    nc.scalar.activation(silu_h[:, :, :], h1n[:, :, :], ACT.Silu).then_inc(
                        act_did["silu"], act_did.next("silu", st, u))

            def round_h(u, i=None):
                act.wait_ge(dve_did["h"], dve_did.at("h", st, u, turn=i, turns=turns))
                nc.scalar.activation(h_hi[:, :, :], h[:, :, :], ACT.Copy).then_inc(act_did["h_hi"], act_did.next("h_hi", st, u))

            def step(s, i=None):
                hi(up_tile(first, s + 1) + 2, i)
                round_h(s, i)
                silu(s + 1, i)
                hi(up_tile(first, s + 1) + 3, i)
                hi(up_tile(first, s + 1) + 4, i)

            hi(first + 2, None)
            if not moe:
                rms_act(act, st)
            silu(0)
            hi(first + 3, None)
            act_did.begin_loop()
            with act.Fori(0, turns) as i:
                step(0, i)
                step(1, i)
            act_did.end_loop(turns)
            act_at.tile += 6 * turns
            if extra:
                step(units - 2)
            used, count = pe_did.tile(down_tile(first, units, units - 2))
            act.wait_ge(used, count)
            round_h(units - 1)
            if st + 1 < len(stages):
                split_hi(act)

        def ffn_dve(dve, st):
            moe, units, turns, extra, first = ffn_sizes(st)

            def lo(n, i):
                if i is None:
                    assert n == dve_at.tile, (n, dve_at.tile)
                    split_lo(dve)
                else:
                    split_lo(dve, i, n)

            def scale_h1(u, i=None):
                if not moe:
                    dve.wait_ge(pe_did["h1"], pe_did.at("h1", st, u, turn=i, turns=turns))
                    if i is not None or u:
                        dve.wait_ge(act_did["silu"], act_did.at("silu", st, u - 1, turn=i, turns=turns))
                    nc.vector.tensor_tensor(h1n[:, :, :], bank(Q[0]), over_pair(rstd[:, :]), ALU.mult).then_inc(
                        dve_did["h1 read"], dve_did.next("h1 read", st, u))

            def gate(u, i=None):
                read = "h1 read" if moe else "silu"
                dve.wait_ge(act_did[read], act_did.at(read, st, u, turn=i, turns=turns))
                if i is not None or u:
                    dve.wait_ge(dve_did["h"], dve_did.at("h", st, u - 1, turn=i, turns=turns))
                if not moe:
                    by = over_pair(rstd[:, :])
                elif i is None:
                    by = over_pair(gates[:, u // 2, :])
                else:
                    by = gates[:, bass.DynSlice(i + u // 2, 1), :].to_broadcast([P, 2, T])
                nc.vector.tensor_tensor(gated[:, :, :], silu_h[:, :, :], by, ALU.mult).then_inc(
                    dve_did["gated"], dve_did.next("gated", st, u))

            def hidden(u, i=None):
                dve.wait_ge(pe_did["h3"], pe_did.at("h3", st, u, turn=i, turns=turns))
                dve.wait_ge(dve_did["gated"], dve_did.at("gated", st, u, turn=i, turns=turns))
                if i is not None or u:
                    dve.wait_ge(dve_did["h_lo"], dve_did.at("h_lo", st, u - 1, turn=i, turns=turns))
                nc.vector.tensor_tensor(h[:, :, :], gated[:, :, :], bank(Q[1]), ALU.mult).then_inc(
                    dve_did["h"], dve_did.next("h", st, u))

            def rest_of_h(u, i=None):
                dve.wait_ge(act_did["h_hi"], act_did.at("h_hi", st, u, turn=i, turns=turns))
                nc.vector.tensor_tensor(h_lo[:, :, :], h[:, :, :], h_hi[:, :, :].bitcast(F32), ALU.subtract).then_inc(
                    dve_did["h_lo"], dve_did.next("h_lo", st, u))

            def step(s, i=None):
                lo(up_tile(first, s + 1) + 2, i)
                rest_of_h(s, i)
                scale_h1(s + 1, i)
                lo(up_tile(first, s + 1) + 3, i)
                gate(s + 1, i)
                hidden(s + 1, i)
                lo(up_tile(first, s + 1) + 4, i)

            lo(first + 2, None)
            if not moe:
                rms_dve(dve, st, Q[3])
            scale_h1(0)
            lo(first + 3, None)
            gate(0)
            hidden(0)
            dve_did.begin_loop()
            with dve.Fori(0, turns) as i:
                step(0, i)
                step(1, i)
            dve_did.end_loop(turns)
            dve_at.tile += 6 * turns
            if extra:
                step(units - 2)
            rest_of_h(units - 1)
            if st + 1 < len(stages):
                split_lo(dve)

        def moe_pe(pe, st):
            li = stages[st][1]
            product(pe, KC, 2, p_hi[:, 2 * li:2 * li + 2, :], p_lo[:, 2 * li:2 * li + 2, :],
                    lambda n: (Y[n // 2], bank(Y[n // 2])[:, n % 2, :]),
                    lambda n: ("ple", st, n // 2) if n % 2 else None,
                    lambda k: pe.wait_ge(dve_did["p_lo"], dve_did.at("p_lo")))
            for i in range(4):
                after(Y[i], ("dve", ("ple part", st, i)))
            before(pe, Q[3])
            pe.wait_ge(dve_did["x_lo"], dve_did.at("x_lo", st - 1, 3))
            for tt in range(2):
                for k in range(KC):
                    at = columns["router_w"] + k * N_EXPERTS
                    last = nc.tensor.matmul(Q[3][:, tt * N_EXPERTS:(tt + 1) * N_EXPERTS], x[:, k, tt * P:(tt + 1) * P],
                                            par[:, at:at + N_EXPERTS], start=(k == 0), stop=(k == KC - 1))
            last.then_inc(pe_did["logits"], pe_did.next("logits", st))
            after(Q[3], ("act", ("router tanh", st)))
            product(pe, KC, KC, x_hi, x_lo, lambda n: (Q[n // 2], bank(Q[n // 2])[:, n % 2, :]),
                    lambda n: ("ple gate", st, n // 2) if n % 2 else None)
            for i in range(4):
                after(Q[i], ("act", ("ple tanh", st, i)))
            pe.wait_ge(dve_did["gates"], dve_did.at("gates", st))
            for j in range(N_EXPERTS // 2):
                b = Q[2 + j % 2]
                before(pe, b)
                for e in range(2):
                    for tt in range(2):
                        at = routing[:, 448 + tt * N_EXPERTS + 2 * j + e:][:, 0:1]
                        last = nc.tensor.matmul(bank(b)[:, e, tt * P:(tt + 1) * P], at.to_broadcast([P, P]),
                                                column("ident", 0, P), start=True, stop=True)
                last.then_inc(pe_did["gates"], pe_did.next("gates", st, j))
                after(b, ("act", ("gate copy", st, j)))

        def moe_act(act, st):
            split_hi(act)
            act.wait_ge(pe_did["logits"], pe_did.at("logits", st))
            nc.scalar.activation(routing[:, 0:32], Q[3][:, 0:32], ACT.Tanh, scale=0.5).then_inc(
                act_did["router tanh"], act_did.next("router tanh", st))
            for i in range(4):
                split_hi(act)
                act.wait_ge(pe_did["ple gate"], pe_did.at("ple gate", st, i))
                nc.scalar.activation(pair(ple_tanh, i), bank(Q[i]), ACT.Tanh, scale=0.5).then_inc(
                    act_did["ple tanh"], act_did.next("ple tanh", st, i))
            for j in range(N_EXPERTS // 2):
                act.wait_ge(pe_did["gates"], pe_did.at("gates", st, j))
                nc.scalar.activation(pair(gates, j), bank(Q[2 + j % 2]), ACT.Copy).then_inc(
                    act_did["gate copy"], act_did.next("gate copy", st, j))

        def route_dve(dve, st):
            E, N = N_EXPERTS, N_EXPERTS // 4
            at = [0]

            def new(*shape):
                size = math.prod(shape)
                ap = routing[:, at[0]:at[0] + size]
                at[0] += size
                assert at[0] <= 448
                return ap.rearrange("p (a b) -> p a b", b=shape[-1])

            def tt(out, a_, b_, op):
                link(dve, "dve", nc.vector.tensor_tensor(out, a_, b_, op))

            def top(v, m, order, hot, key):
                link(dve, "dve", nc.vector.tensor_reduce(m[:, :, 0], v, AX.X, ALU.max))
                tt(hot, v, m[:, :, 0:1].to_broadcast([P, 2, v.shape[2]]), ALU.is_equal)
                tt(key, hot, order, ALU.mult)
                link(dve, "dve", nc.vector.tensor_reduce(m[:, :, 0], key, AX.X, ALU.max))
                tt(hot, key, m[:, :, 0:1].to_broadcast([P, 2, v.shape[2]]), ALU.is_equal)

            score, sel = new(2, E), new(2, E)
            high, low, best, second = new(8, 2), new(8, 2), new(8, 1), new(8, 1)
            group, hot_g, key_g, m = new(2, 4), new(2, 4), new(2, 4), new(2, 1)
            hot, hot2, key, masked = new(2, E), new(2, E), new(2, E), new(2, E)
            dve.wait_ge(act_did["router tanh"], act_did.at("router tanh", st))
            link(dve, "dve", nc.vector.tensor_scalar(score, score, 0.5, 0.5, ALU.mult, ALU.add))
            tt(sel, score, column("router_bias", 0, E).unsqueeze(1).to_broadcast([P, 2, E]), ALU.add)
            quads = sel.rearrange("p a (g c d) -> p (a g) c d", c=2, d=2)
            tt(high, quads[:, :, :, 0], quads[:, :, :, 1], ALU.max)
            tt(low, quads[:, :, :, 0], quads[:, :, :, 1], ALU.min)
            tt(best[:, :, 0], high[:, :, 0], high[:, :, 1], ALU.max)
            tt(high[:, :, 0], high[:, :, 0], high[:, :, 1], ALU.min)
            tt(low[:, :, 0], low[:, :, 0], low[:, :, 1], ALU.max)
            tt(second[:, :, 0], high[:, :, 0], low[:, :, 0], ALU.max)
            tt(group.rearrange("p a b -> p (a b)"), best[:, :, 0], second[:, :, 0], ALU.add)
            top(group, m, column("order", 0, 4).unsqueeze(1).to_broadcast([P, 2, 4]), hot_g, key_g)
            spread = hot_g.rearrange("p a b -> p (a b)").unsqueeze(2).to_broadcast([P, 8, N])
            flat = lambda ap: ap.rearrange("p a (g c) -> p (a g) c", c=N)
            tt(flat(masked), flat(sel), spread, ALU.mult)
            link(dve, "dve", nc.vector.tensor_scalar(hot_g, hot_g, NEG, -NEG, ALU.mult, ALU.add))
            tt(flat(masked), flat(masked), spread, ALU.add)
            order = column("order", 4, E).unsqueeze(1).to_broadcast([P, 2, E])
            top(masked, m, order, hot, key)
            link(dve, "dve", nc.vector.scalar_tensor_tensor(masked, hot, -2.0 * NEG, masked, ALU.mult, ALU.add))
            top(masked, m, order, hot2, key)
            tt(hot, hot, hot2, ALU.add)
            tt(hot, hot, score, ALU.mult)
            link(dve, "dve", nc.vector.tensor_reduce(m[:, :, 0], hot, AX.X, ALU.add))
            link(dve, "dve", nc.vector.reciprocal(m[:, :, 0], m[:, :, 0]))
            out = routing[:, 448:480].rearrange("p (a b) -> p a b", b=E)
            nc.vector.tensor_tensor(out, hot, m[:, :, 0:1].to_broadcast([P, 2, E]), ALU.mult).then_inc(
                dve_did["gates"], dve_did.next("gates", st))

        def moe_dve(dve, st):
            split_lo(dve)
            route_dve(dve, st)
            for i in range(4):
                split_lo(dve)
                link(dve, "dve", nc.vector.tensor_scalar(pair(x_alpha, i), pair(x, i), ALPHA, None, ALU.mult))
                dve.wait_ge(pe_did["ple"], pe_did.at("ple", st, i))
                dve.wait_ge(act_did["ple tanh"], act_did.at("ple tanh", st, i))
                nc.vector.scalar_tensor_tensor(ple_part, pair(ple_tanh, i), 1.0, bank(Y[i]), ALU.add, ALU.mult).then_inc(
                    dve_did["ple part"], dve_did.next("ple part", st, i))
                dve.wait_ge(dve_did["ple part"], dve_did.at("ple part", st, i))
                link(dve, "dve", nc.vector.scalar_tensor_tensor(pair(x_alpha, i), ple_part, 0.5, pair(x_alpha, i), ALU.mult, ALU.add))
            dve.wait_ge(act_did["gate copy"], act_did.at("gate copy", st, N_EXPERTS // 2 - 1))

        def outer_pe(pe, st, ks):
            product(pe, KC, ks, c_hi, c_lo, lambda n: (Y[n // 2], bank(Y[n // 2])[:, n % 2, :]),
                    lambda n: ("y", st, n // 2) if n % 2 else None,
                    lambda k: pe.wait_ge(dve_did["c_lo"], dve_did.at("c_lo", st, k // 2)))
            for i in range(4):
                after(Y[i], ("dve", ("z" if stages[st][0] in LN_STAGES else "x", st, i)))
            end_stream_stage(pe, st)

        def round_c(act, st, i, src, who, label):
            act.wait_ge(did[who][label[0]], did[who].at(*label))
            nc.scalar.activation(pair(c_hi, i), src, ACT.Copy).then_inc(act_did["c_hi"], act_did.next("c_hi", st, i))

        def rest_of_c(dve, st, i, src):
            dve.wait_ge(act_did["c_hi"], act_did.at("c_hi", st, i))
            nc.vector.tensor_tensor(pair(c_lo, i), src, pair(c_hi, i).bitcast(F32), ALU.subtract).then_inc(
                dve_did["c_lo"], dve_did.next("c_lo", st, i))

        conv_u = region(0, KC, T + 2)
        conv_c = region(2100, 2, T)
        conv_y = region(2700, 2, T)
        conv_b = region(3300, 2, T)
        conv_out = region(4096, KC, T)

        def conv_bank(f):
            return psum[f % 8]

        def conv_pe(pe, st):
            for i in range(4):
                for j, name in enumerate(("conv c", "conv h", "conv b")):
                    f = 3 * i + j
                    b = conv_bank(f)
                    product(pe, 2, KC, x_hi, x_lo, lambda n: (b, bank(b)[:, n, :]),
                            lambda n: (name, st, i) if n else None, input_ready(pe, st) if f == 0 else None)
                    after(b, ("dve", (name, st, i)))
                    if f == 0:
                        rms_pe(pe, st, Y[3])
            outer_pe(pe, st, KC)

        def conv_act(act, st):
            split_hi(act)
            rms_act(act, st)
            for i in range(4):
                for _ in range(3):
                    split_hi(act)
                round_c(act, st, i, pair(conv_out, i), "dve", ("conv out", st, i))
            for _ in range(3):
                split_hi(act)

        def conv_dve(dve, st):
            split_lo(dve)
            link(dve, "dve", nc.vector.memset(conv_u[:, :, 0:2], 0.0))
            rms_dve(dve, st, Y[3])
            link(dve, "dve", nc.vector.tensor_tensor(tmp_r[:, :], rstd[:, :], rstd[:, :], ALU.mult))
            for i in range(4):
                c, h_, b = (bank(conv_bank(3 * i + j)) for j in range(3))
                dve.wait_ge(pe_did["conv c"], pe_did.at("conv c", st, i))
                nc.vector.tensor_tensor(conv_c, c, over_pair(tmp_r[:, :]), ALU.mult).then_inc(
                    dve_did["conv c"], dve_did.next("conv c", st, i))
                split_lo(dve)
                dve.wait_ge(dve_did["conv c"], dve_did.at("conv c", st, i))
                dve.wait_ge(pe_did["conv h"], pe_did.at("conv h", st, i))
                nc.vector.tensor_tensor(conv_u[:, 2 * i:2 * i + 2, 2:], conv_c, h_, ALU.mult).then_inc(
                    dve_did["conv h"], dve_did.next("conv h", st, i))
                split_lo(dve)
                dve.wait_ge(dve_did["conv h"], dve_did.at("conv h", st, i))
                w = lambda tap, k: column("conv_w", 24 * stages[st][1] + 8 * tap + k)
                for tap in range(3):
                    for k in (2 * i, 2 * i + 1):
                        src, dst = conv_u[:, k, tap:tap + T], conv_y[:, k % 2, :]
                        if tap == 0:
                            last = nc.vector.tensor_scalar(dst, src, w(tap, k), None, ALU.mult)
                        else:
                            last = nc.vector.scalar_tensor_tensor(dst, src, w(tap, k), dst, ALU.mult, ALU.add)
                    link(dve, "dve", last)
                dve.wait_ge(pe_did["conv b"], pe_did.at("conv b", st, i))
                nc.vector.tensor_tensor(conv_b, b, over_pair(rstd[:, :]), ALU.mult).then_inc(
                    dve_did["conv b"], dve_did.next("conv b", st, i))
                dve.wait_ge(dve_did["conv b"], dve_did.at("conv b", st, i))
                nc.vector.tensor_tensor(pair(conv_out, i), conv_b, conv_y, ALU.mult).then_inc(
                    dve_did["conv out"], dve_did.next("conv out", st, i))
                split_lo(dve)
                rest_of_c(dve, st, i, pair(conv_out, i))
            for _ in range(3):
                split_lo(dve)

        SB_HEADS, SB_DIM, WIDE = 16, 64, T + P
        sb_q = region(0, KC, T)
        sb_k = region(2048, KC, T)
        sb_v = region(4096, 2, D)
        sb_log = region(6144, 2, WIDE)
        sb_soft = region(6912, 2, WIDE)
        sb_w = region(7680, 2, WIDE)

        def token_product(pe, st, ks, xh, xl, name):
            for half in range(2):
                for tt in range(2):
                    before(pe, psum[2 * half + tt])
                for k in range(ks):
                    places = [next_block(pe) for _ in range(4)]
                    t, b = places[0]
                    cols = slice(b * P, (b + 4) * P)
                    for tt in range(2):
                        out = psum[2 * half + tt][:, :]
                        xs_ = slice(tt * P, (tt + 1) * P)
                        nc.tensor.matmul(out, xh[:, k, xs_], w_hi[:, t % RING, cols], start=(k == 0), stop=False)
                        nc.tensor.matmul(out, xh[:, k, xs_], w_lo[:, t % RING, cols], start=False, stop=False)
                        last = nc.tensor.matmul(out, xl[:, k, xs_], w_hi[:, t % RING, cols], start=False, stop=(k == ks - 1))
                        signal_product(last, (name, st, 2 * half + tt) if k == ks - 1 else None, t, places[-1][1] if tt else 0)
            for i in range(4):
                after(psum[i], ("dve", (name + " copy", st, i)))

        def sb_rows(h_):
            return slice(SB_DIM * (h_ % 2), SB_DIM * (h_ % 2) + SB_DIM)

        def sb_pe(pe, st):
            product(pe, 2 * KC, KC, x_hi, x_lo, lambda n: (psum[n // 2], bank(psum[n // 2])[:, n % 2, :]),
                    lambda n: ("qk", st, n // 2) if n % 2 else None, input_ready(pe, st))
            for f in range(8):
                after(psum[f], ("act", ("q", st, f)) if f < 4 else ("dve", ("k", st, f)))
            token_product(pe, st, KC, x_hi, x_lo, "v")

            def scores(h_):
                b, r, c = Q[h_ % 4], sb_rows(h_), h_ // 2
                before(pe, b)
                if h_ == 0:
                    pe.wait_ge(act_did["q"], act_did.at("q", st, 3))
                    pe.wait_ge(dve_did["k"], dve_did.at("k", st, 7))
                nc.tensor.matmul(b[:, 0:T], sb_k[r, c, 0:P], sb_q[r, c, :], start=True, stop=True, skip_group_check=True)
                nc.tensor.matmul(b[:, T:WIDE], sb_k[r, c, P:T], sb_q[r, c, P:T], start=False, stop=True, skip_group_check=True).then_inc(
                    pe_did["scores"], pe_did.next("scores", st, h_))

            def log_weights(h_):
                b, soft = Q[h_ % 4], sb_soft[:, h_ % 2, :]
                pe.wait_ge(dve_did["softplus"], dve_did.at("softplus", st, h_))
                pe.wait_ge(act_did["log"], act_did.at("log", st, h_))
                add = dict(start=False, stop=True, skip_group_check=True)
                nc.tensor.matmul(b[:, 0:T], column("minus_tri", 0, P), soft[:, 0:T], **add)
                nc.tensor.matmul(b[:, P:T], column("minus_ones", 0, P), soft[:, T:WIDE], **add)
                nc.tensor.matmul(b[:, T:WIDE], column("minus_tri", 0, P), soft[:, T:WIDE], **add)
                nc.tensor.matmul(b[:, 0:P], column("ident", 0, P), column("future", 0, P), **add)
                nc.tensor.matmul(b[:, T:WIDE], column("ident", 0, P), column("future", 0, P), **add).then_inc(
                    pe_did["log weights"], pe_did.next("log weights", st, h_))
                after(b, ("act", ("weights", st, h_)))

            def values(h_):
                b, r, w = psum[4 + h_ // 4], sb_rows(h_), sb_w[:, h_ % 2, :]
                if h_ % 4 == 0:
                    before(pe, b)
                pe.wait_ge(act_did["weights"], act_did.at("weights", st, h_))
                if h_ == 0:
                    pe.wait_ge(dve_did["v copy"], dve_did.at("v copy", st, 3))
                out = bank(b)[r, h_ // 2 % 2, :]
                cols = slice(h_ * SB_DIM, (h_ + 1) * SB_DIM)
                nc.tensor.matmul(out, sb_v[:, 0, cols], w[:, 0:T], start=True, stop=False, skip_group_check=True)
                nc.tensor.matmul(out[:, P:T], sb_v[:, 1, cols], w[:, T:WIDE], start=False, stop=True, skip_group_check=True).then_inc(
                    pe_did["values"], pe_did.next("values", st, h_))

            for n in range(SB_HEADS + 2):
                if n < SB_HEADS:
                    scores(n)
                if 0 < n <= SB_HEADS:
                    log_weights(n - 1)
                if n > 1:
                    values(n - 2)
            for i in range(4):
                after(psum[4 + i], ("dve", ("c_lo", st, i)))
            outer_pe(pe, st, KC)

        def sb_act(act, st):
            for f in range(4):
                split_hi(act)
                act.wait_ge(pe_did["qk"], pe_did.at("qk", st, f))
                nc.scalar.activation(pair(sb_q, f), bank(psum[f]), ACT.Copy, scale=SB_DIM ** -0.5).then_inc(
                    act_did["q"], act_did.next("q", st, f))
            for _ in range(9):
                split_hi(act)
            nc.scalar.preload_act_table_set("natural_log_exp_and_others")
            for n in range(SB_HEADS + 2):
                if n < SB_HEADS:
                    log = sb_log[:, n % 2, :]
                    act.wait_ge(pe_did["scores"], pe_did.at("scores", st, n))
                    if n > 1:
                        act.wait_ge(dve_did["softplus"], dve_did.at("softplus", st, n - 2))
                    link(act, "act", nc.scalar.activation(log, Q[n % 4][:, 0:WIDE], ACT.Abs))
                    link(act, "act", nc.scalar.activation(log, log, ACT.Exp, scale=-1.0))
                    nc.scalar.activation(log, log, ACT.Ln, bias=1.0).then_inc(act_did["log"], act_did.next("log", st, n))
                if 0 < n <= SB_HEADS:
                    act.wait_ge(pe_did["log weights"], pe_did.at("log weights", st, n - 1))
                    if n > 2:
                        act.wait_ge(pe_did["values"], pe_did.at("values", st, n - 3))
                    nc.scalar.activation(sb_w[:, (n - 1) % 2, :], Q[(n - 1) % 4][:, 0:WIDE], ACT.Exp).then_inc(
                        act_did["weights"], act_did.next("weights", st, n - 1))
                if n > 1 and (n - 2) % 4 == 3:
                    i = (n - 2) // 4
                    round_c(act, st, i, bank(psum[4 + i]), "pe", ("values", st, n - 2))
            for _ in range(3):
                split_hi(act)

        def sb_dve(dve, st):
            for _ in range(4):
                split_lo(dve)
            for f in range(4, 8):
                split_lo(dve)
                dve.wait_ge(pe_did["qk"], pe_did.at("qk", st, f))
                nc.vector.tensor_copy(pair(sb_k, f - 4), bank(psum[f])).then_inc(dve_did["k"], dve_did.next("k", st, f))
            for half in range(2):
                split_lo(dve)
                split_lo(dve)
                for tt in range(2):
                    dve.wait_ge(pe_did["v"], pe_did.at("v", st, 2 * half + tt))
                    nc.vector.tensor_copy(sb_v[:, tt, half * 512:(half + 1) * 512], psum[2 * half + tt][:, :]).then_inc(
                        dve_did["v copy"], dve_did.next("v copy", st, 2 * half + tt))
            split_lo(dve)
            for n in range(SB_HEADS + 2):
                if n < SB_HEADS:
                    soft = sb_soft[:, n % 2, :]
                    dve.wait_ge(act_did["log"], act_did.at("log", st, n))
                    if n > 1:
                        dve.wait_ge(pe_did["log weights"], pe_did.at("log weights", st, n - 2))
                    link(dve, "dve", nc.vector.scalar_tensor_tensor(soft, Q[n % 4][:, 0:WIDE], 0.0, sb_log[:, n % 2, :], ALU.max, ALU.add))
                    for at in (0, T):
                        last = nc.vector.tensor_tensor(soft[:, at:at + P], soft[:, at:at + P], column("strict", 0, P), ALU.mult)
                    last.then_inc(dve_did["softplus"], dve_did.next("softplus", st, n))
                if n > 1 and (n - 2) % 4 == 3:
                    i = (n - 2) // 4
                    rest_of_c(dve, st, i, bank(psum[4 + i]))
            for _ in range(3):
                split_lo(dve)

        LC = LRU_CHUNKS
        LG = LC // 2
        lru_in = region(0, LC, T + 3)
        lru_a = region(0, LC, T)
        lru_gate = region(2600, LC, T)
        lru_x = region(5160, LC, T)
        lru_r = region(7720, LC, T)
        lru_i = region(10280, LC, T)
        half_bias = small[:, 0:2 * LC]
        decay = small[:, 2 * LC:3 * LC]

        def lru_gate_fill(g):
            return 5 if g == 0 else 15 + g

        def lru_pe(pe, st):
            def fill(name, g, f, first=False):
                b = psum[f % 8]
                product(pe, 2, KC, x_hi, x_lo, lambda n: (b, bank(b)[:, n, :]), lambda n: (name, st, g) if n else None,
                        input_ready(pe, st) if first else None)
                after(b, ("dve", (name, st, g)))

            for g in range(LG):
                fill("rec", g, g, g == 0)
                if g == 0:
                    rms_pe(pe, st, psum[7])
            fill("gate", 0, 5)
            for g in range(LG):
                pe.wait_ge(dve_did["inner lo"], dve_did.at("inner lo", st, g))
                for j, name in enumerate(("r", "i")):
                    b = psum[(6 + 2 * g + j) % 8]
                    before(pe, b)
                    for n in range(2):
                        t, place = next_block(pe)
                        hi, lo = block_of(t, place)
                        last = three(bank(b)[:, n, :], hi, lo, c_hi[:, 2 * g + n, :], c_lo[:, 2 * g + n, :], True, True)
                        signal_product(last, (name, st, g) if n else None, t, place)
                    after(b, ("act", (name, st, g)))
            for g in range(1, LG):
                fill("gate", g, lru_gate_fill(g))
            outer_pe(pe, st, LC)

        def lru_act(act, st):
            split_hi(act)
            rms_act(act, st)
            link(act, "act", nc.scalar.activation(small[:, 32:32 + LC], column("lru_lam", 0, LC), ACT.Abs))
            nc.scalar.activation(small[:, 32:32 + LC], small[:, 32:32 + LC], ACT.Exp, scale=-1.0).then_inc(
                act_did["lam"], act_did.next("lam", st))
            for g in range(LG):
                split_hi(act)
                act.wait_ge(dve_did["convolved"], dve_did.at("convolved", st, g))
                nc.scalar.activation(pair(c_hi, g), pair(lru_x, g), ACT.Copy).then_inc(
                    act_did["inner hi"], act_did.next("inner hi", st, g))
            split_hi(act)
            split_hi(act)
            act.wait_ge(dve_did["half bias"], dve_did.at("half bias", st))
            for g in range(LG):
                for j, (name, dst) in enumerate((("r", lru_r), ("i", lru_i))):
                    act.wait_ge(pe_did[name], pe_did.at(name, st, g))
                    for n in range(2):
                        c = 2 * g + n
                        last = nc.scalar.activation(dst[:, c, :], bank(psum[(6 + 2 * g + j) % 8])[:, n, :], ACT.Tanh,
                                                    bias=half_bias[:, j * LC + c:j * LC + c + 1], scale=0.5)
                    last.then_inc(act_did[name], act_did.next(name, st, g))
                if g in (1, 4):
                    split_hi(act)
            for g in range(LG):
                act.wait_ge(dve_did["log a"], dve_did.at("log a", st, g))
                link(act, "act", nc.scalar.activation(pair(lru_a, g), pair(lru_r, g), ACT.Exp))
                nc.scalar.activation(pair(lru_r, g), pair(lru_r, g), ACT.Tanh).then_inc(act_did["a"], act_did.next("a", st, g))
                if g < 2:
                    split_hi(act)
            for g in range(LG):
                act.wait_ge(dve_did["minus b2"], dve_did.at("minus b2", st, g))
                nc.scalar.activation(pair(lru_x, g), pair(lru_x, g), ACT.Sqrt, scale=-1.0).then_inc(
                    act_did["root"], act_did.next("root", st, g))
            for g in range(LG):
                act.wait_ge(dve_did["gate"], dve_did.at("gate", st, g))
                nc.scalar.activation(pair(lru_gate, g), pair(lru_gate, g), ACT.Gelu_apprx_tanh).then_inc(
                    act_did["gelu"], act_did.next("gelu", st, g))
            for g in range(LG):
                round_c(act, st, g, pair(lru_x, g), "dve", ("gated", st, g))
            for _ in range(5):
                split_hi(act)

        def lru_dve(dve, st):
            def v(ins):
                link(dve, "dve", ins)

            split_lo(dve)
            v(nc.vector.memset(lru_in[:, :, 0:3], 0.0))
            rms_dve(dve, st, psum[7])
            for g in range(LG):
                dve.wait_ge(pe_did["rec"], pe_did.at("rec", st, g))
                nc.vector.tensor_tensor(lru_in[:, 2 * g:2 * g + 2, 3:], bank(psum[g]), over_pair(rstd[:, :]), ALU.mult).then_inc(
                    dve_did["rec"], dve_did.next("rec", st, g))
                dve.wait_ge(dve_did["rec"], dve_did.at("rec", st, g))
                split_lo(dve)
                for tap in range(4):
                    for c in (2 * g, 2 * g + 1):
                        src, dst, w = lru_in[:, c, tap:tap + T], lru_x[:, c, :], column("lru_conv_w", tap * LC + c)
                        if tap == 0:
                            last = nc.vector.tensor_scalar(dst, src, w, column("lru_conv_b", c), ALU.mult, ALU.add)
                        else:
                            last = nc.vector.scalar_tensor_tensor(dst, src, w, dst, ALU.mult, ALU.add)
                    if tap < 3:
                        v(last)
                last.then_inc(dve_did["convolved"], dve_did.next("convolved", st, g))
                dve.wait_ge(dve_did["convolved"], dve_did.at("convolved", st, g))
                dve.wait_ge(act_did["inner hi"], act_did.at("inner hi", st, g))
                nc.vector.tensor_tensor(pair(c_lo, g), pair(lru_x, g), pair(c_hi, g).bitcast(F32), ALU.subtract).then_inc(
                    dve_did["inner lo"], dve_did.next("inner lo", st, g))

            def gate(g):
                dve.wait_ge(pe_did["gate"], pe_did.at("gate", st, g))
                nc.vector.tensor_tensor(pair(lru_gate, g), bank(psum[lru_gate_fill(g) % 8]), over_pair(rstd[:, :]), ALU.mult).then_inc(
                    dve_did["gate"], dve_did.next("gate", st, g))
            split_lo(dve)
            gate(0)
            v(nc.vector.tensor_scalar(half_bias[:, 0:LC], column("lru_ba", 0, LC), 0.5, None, ALU.mult))
            nc.vector.tensor_scalar(half_bias[:, LC:2 * LC], column("lru_bx", 0, LC), 0.5, None, ALU.mult).then_inc(
                dve_did["half bias"], dve_did.next("half bias", st))
            split_lo(dve)
            dve.wait_ge(act_did["lam"], act_did.at("lam", st))
            e, s_, s2, acc = (small[:, 32 + j * LC:32 + (j + 1) * LC] for j in range(4))
            v(nc.vector.tensor_scalar(s_, e, 2.0, None, ALU.add))
            v(nc.vector.reciprocal(s_, s_))
            v(nc.vector.tensor_tensor(s_, s_, e, ALU.mult))
            v(nc.vector.tensor_tensor(s2, s_, s_, ALU.mult))
            v(nc.vector.tensor_scalar(acc, s2, 1.0 / 17.0, None, ALU.mult))
            for odd in range(15, 1, -2):
                v(nc.vector.scalar_tensor_tensor(acc, acc, 1.0 / odd, s2, ALU.add, ALU.mult))
            v(nc.vector.scalar_tensor_tensor(acc, acc, 1.0, s_, ALU.add, ALU.mult))
            v(nc.vector.tensor_scalar(e, column("lru_lam", 0, LC), 0.0, 4.0, ALU.min, ALU.mult))
            v(nc.vector.scalar_tensor_tensor(decay, acc, -8.0, e, ALU.mult, ALU.add))
            for g in range(LG):
                dve.wait_ge(act_did["r"], act_did.at("r", st, g))
                nc.vector.scalar_tensor_tensor(pair(lru_r, g), pair(lru_r, g), 1.0, over_tokens(decay[:, 2 * g:2 * g + 2]), ALU.add, ALU.mult).then_inc(
                    dve_did["log a"], dve_did.next("log a", st, g))
                dve.wait_ge(act_did["i"], act_did.at("i", st, g))
                v(nc.vector.scalar_tensor_tensor(pair(lru_i, g), pair(lru_i, g), 1.0, pair(lru_x, g), ALU.add, ALU.mult))
                if g in (1, 4):
                    split_lo(dve)
            for g in range(LG):
                dve.wait_ge(act_did["a"], act_did.at("a", st, g))
                v(nc.vector.tensor_tensor(pair(lru_x, g), pair(lru_a, g), pair(lru_a, g), ALU.mult))
                nc.vector.scalar_tensor_tensor(pair(lru_x, g), pair(lru_x, g), 1.0, pair(lru_r, g), ALU.add, ALU.mult).then_inc(
                    dve_did["minus b2"], dve_did.next("minus b2", st, g))
                if g < 3:
                    gate(g + 1)
                if g < 2:
                    split_lo(dve)
            gate(4)
            v(nc.vector.memset(lru_a[:, :, 0:1], 0.0))
            for g in range(LG):
                dve.wait_ge(act_did["root"], act_did.at("root", st, g))
                v(nc.vector.scalar_tensor_tensor(pair(lru_i, g), pair(lru_x, g), 0.5, pair(lru_i, g), ALU.mult, ALU.mult))
                flat = lambda ap: pair(ap, g).rearrange("p a t -> p (a t)")
                v(nc.vector.tensor_tensor_scan(flat(lru_r), flat(lru_a), flat(lru_i), 0.0, ALU.mult, ALU.add))
                dve.wait_ge(act_did["gelu"], act_did.at("gelu", st, g))
                nc.vector.tensor_tensor(pair(lru_x, g), pair(lru_gate, g), pair(lru_r, g), ALU.mult).then_inc(
                    dve_did["gated"], dve_did.next("gated", st, g))
            for g in range(LG):
                rest_of_c(dve, st, g, pair(lru_x, g))
            for _ in range(5):
                split_lo(dve)

        TURN_1 = 6.28125
        TURN_2 = float(np.float32(math.floor((TWO_PI - TURN_1) * 2 ** 21) / 2 ** 21))
        TURN_3 = TWO_PI - TURN_1 - TURN_2
        NEARLY_PI = 3.1415925

        def reduce_angle(dve, angle, turns, label):
            link(dve, "dve", nc.vector.tensor_scalar(turns, angle, 1.0 / TWO_PI, ROUND, ALU.mult, ALU.add))
            link(dve, "dve", nc.vector.tensor_scalar(turns, turns, ROUND, None, ALU.subtract))
            for part in (TURN_1, TURN_2, TURN_3):
                link(dve, "dve", nc.vector.scalar_tensor_tensor(angle, turns, -part, angle, ALU.mult, ALU.add))
            nc.vector.tensor_scalar(angle, angle, NEARLY_PI, -NEARLY_PI, ALU.min, ALU.max).then_inc(
                dve_did[label[0]], dve_did.next(*label))

        def sine_act(act, angle, size, sine, cosine, label):
            link(act, "act", nc.scalar.activation(size, angle, ACT.Abs))
            nc.scalar.activation(sine, angle, ACT.Sin)
            nc.scalar.activation(cosine, size, ACT.Sin, bias=column("half_pi"), scale=-1.0).then_inc(
                act_did[label[0]], act_did.next(*label))

        HEADS = 8
        WIDE = T + P
        QK_SCALE = 1.0 / math.sqrt(192.0)
        latent = region(0, 7, T)
        latent_sq = region(1800, 7, T)
        latent_var = region(3848, 3, T)
        latent_r = region(4616, 3, T)
        latent_t = region(5384, 3, T)
        m_q = region(0, HEADS, T)
        m_k = region(2048, HEADS, T)
        m_v = region(4096, 2, D)
        m_kr = region(6144, 4, 2, T)
        m_qr = region(8192, 2, 2, T)
        cosine, sine = region(9216, T), region(9472, T)
        angle, turns_ = region(9728, T), region(9984, T)
        m_sq = region(10240, 2, 2, T)
        m_var, m_r, m_t = region(11264, 2, T), region(11776, 2, T), region(12288, 2, T)
        m_p, m_pt = region(10240, 2, WIDE), region(11008, 2, WIDE)
        PAIRS = 9

        def m_bank(p, what):
            if p == 0:
                return psum[{"raw": 0, "raw2": 1, "sum": 2}[what]]
            return psum[(2 * p + 1 + (what == "sum")) % 8]

        def mla_pe(pe, st):
            product(pe, 7, KC, x_hi, x_lo, lambda n: (psum[n // 2], bank(psum[n // 2])[:, n % 2, :]),
                    lambda n: ("down", st, n // 2) if n % 2 or n == 6 else None, input_ready(pe, st))
            for f in range(4):
                after(psum[f], ("dve", ("latent", st, f)))
            rms_pe(pe, st, psum[7])
            for f in range(4):
                pe.wait_ge(act_did["latent squared"], act_did.at("latent squared", st, f))
            for out, weights, cs in ((bank(psum[4])[:, 0, :], ones[:, :], (0, 1, 2)), (bank(psum[4])[:, 1, :], ones[:, :], (3, 4)),
                                     (bank(psum[5])[:, 0, :], column("quarter", 0, P), (5, 6))):
                if cs[0] in (0, 5):
                    before(pe, psum[4 + cs[0] // 5])
                for c in cs:
                    last = nc.tensor.matmul(out, weights, latent_sq[:, c, :], start=(c == cs[0]), stop=(c == cs[-1]))
            last.then_inc(pe_did["latent sums"], pe_did.next("latent sums", st))
            for b in (psum[4], psum[5]):
                after(b, ("dve", ("latent variance", st)))
            q_in = c_hi[:, 0:3, :], c_lo[:, 0:3, :]
            kv_in = c_hi[:, 3:5, :], c_lo[:, 3:5, :]

            def raw_pair(p):
                xh, xl = q_in if p < 5 else kv_in
                for what in (("raw", "raw2") if p == 0 else ("raw",)):
                    b = m_bank(p, what)
                    product(pe, 2, 3 if p < 5 else 2, xh, xl, lambda n: (b, bank(b)[:, n, :]),
                            lambda n: (what, st, p) if n else None,
                            (lambda k: pe.wait_ge(dve_did["latent lo"], dve_did.at("latent lo", st))) if (p, what) == (0, "raw") else None)
                    after(b, ("dve", ("normed pair", st, p)))

            def sum_pair(p):
                b = m_bank(p, "sum")
                before(pe, b)
                pe.wait_ge(act_did["squared pair"], act_did.at("squared pair", st, p))
                if p == 0:
                    for n in range(2):
                        for half in range(2):
                            last = nc.tensor.matmul(bank(b)[:, n, :], column("quarter", 0, P), m_sq[:, half, n, :],
                                                    start=(half == 0), stop=(half == 1))
                else:
                    last = nc.tensor.matmul(b[:, :], ones[:, :], m_sq[:, p % 2, :, :].rearrange("p a t -> p (a t)"), start=True, stop=True)
                last.then_inc(pe_did["pair sums"], pe_did.next("pair sums", st, p))
                after(b, ("dve", ("pair variance", st, p)))

            raw_pair(0)
            for p in range(PAIRS):
                if p + 1 < PAIRS:
                    raw_pair(p + 1)
                sum_pair(p)
            token_product(pe, st, 2, kv_in[0], kv_in[1], "mla v")

            def scores(n):
                b = Q[n % 2]
                before(pe, b)
                if n == 0:
                    pe.wait_ge(dve_did["rope"], dve_did.at("rope", st))
                    pe.wait_ge(dve_did["normed pair"], dve_did.at("normed pair", st, PAIRS - 1))
                g = n // 4
                for out, qs, ks_ in ((b[:, 0:P], slice(0, P), slice(0, P)), (b[:, P:WIDE], slice(P, T), slice(0, T))):
                    nc.tensor.matmul(out, m_q[:, n, qs], m_k[:, n, ks_], start=qs.start == 0, stop=True, skip_group_check=True)
                    for half in range(2):
                        nc.tensor.matmul(out, m_qr[:, half, g, qs], m_kr[:, n % 4, half, ks_], start=False, stop=True, skip_group_check=True)
                nc.tensor.matmul(b[:, 0:P], column("ident", 0, P), column("causal", 0, P), start=False, stop=True, skip_group_check=True)
                nc.tensor.matmul(b[:, T:WIDE], column("ident", 0, P), column("causal", 0, P), start=False, stop=True, skip_group_check=True).then_inc(
                    pe_did["scores"], pe_did.next("scores", st, n))
                after(b, ("act", ("exp", st, n)))

            def turn(n):
                b = Q[2 + n % 2]
                before(pe, b)
                pe.wait_ge(dve_did["probabilities"], dve_did.at("probabilities", st, n))
                for j in range(3):
                    s_ = slice(j * P, (j + 1) * P)
                    last = nc.tensor.transpose(b[:, s_], m_p[:, n % 2, s_], column("ident", 0, P))
                last.then_inc(pe_did["turned"], pe_did.next("turned", st, n))
                after(b, ("act", ("turned copy", st, n)))

            def values(n):
                b = Y[n // 2]
                if n % 2 == 0:
                    before(pe, b)
                pe.wait_ge(act_did["turned copy"], act_did.at("turned copy", st, n))
                if n == 0:
                    pe.wait_ge(dve_did["mla v copy"], dve_did.at("mla v copy", st, 3))
                out, w = bank(b)[:, n % 2, :], m_pt[:, n % 2, :]
                nc.tensor.matmul(out, m_v[:, 0, n * P:(n + 1) * P], w[:, 0:T], start=True, stop=True, skip_group_check=True)
                nc.tensor.matmul(out[:, P:T], m_v[:, 1, n * P:(n + 1) * P], w[:, T:WIDE], start=False, stop=True, skip_group_check=True).then_inc(
                    pe_did["values"], pe_did.next("values", st, n))

            for n in range(HEADS + 2):
                if n < HEADS:
                    scores(n)
                if 0 < n <= HEADS:
                    turn(n - 1)
                if n > 1:
                    values(n - 2)
            for i in range(4):
                after(Y[i], ("dve", ("c_lo", st, i)))
            outer_pe(pe, st, KC)

        def mla_act(act, st):
            split_hi(act)
            for _ in range(3):
                split_hi(act)
            rms_act(act, st)
            for f in range(4):
                act.wait_ge(dve_did["latent"], dve_did.at("latent", st, f))
                cs = slice(2 * f, min(2 * f + 2, 7))
                nc.scalar.activation(latent_sq[:, cs, :], latent[:, cs, :], ACT.Square).then_inc(
                    act_did["latent squared"], act_did.next("latent squared", st, f))
            nc.scalar.preload_act_table_set("natural_log_exp_and_others")
            act.wait_ge(dve_did["latent variance"], dve_did.at("latent variance", st))
            rsqrt_act(act, latent_var, latent_r, ("latent seed", st))
            act.wait_ge(dve_did["latent normed"], dve_did.at("latent normed", st))
            nc.scalar.activation(c_hi[:, 0:5, :], latent[:, 0:5, :], ACT.Copy).then_inc(
                act_did["latent hi"], act_did.next("latent hi", st))
            act.wait_ge(dve_did["angle"], dve_did.at("angle", st))
            sine_act(act, angle, turns_, sine, cosine, ("rotation", st))
            split_hi(act)
            nc.scalar.preload_act_table_set("natural_log_exp_and_others")
            for p in range(PAIRS):
                sq = m_sq[:, p % 2, :, :]
                if p == 0:
                    for half, what in enumerate(("raw", "raw2")):
                        act.wait_ge(pe_did[what], pe_did.at(what, st, 0))
                        last = nc.scalar.activation(m_sq[:, half, :, :], bank(m_bank(0, what)), ACT.Square)
                else:
                    act.wait_ge(pe_did["raw"], pe_did.at("raw", st, p))
                    act.wait_ge(pe_did["pair sums"], pe_did.at("pair sums", st, max(p - 2, 0)))
                    last = nc.scalar.activation(sq, bank(m_bank(p, "raw")), ACT.Square)
                last.then_inc(act_did["squared pair"], act_did.next("squared pair", st, p))
                act.wait_ge(dve_did["pair variance"], dve_did.at("pair variance", st, p))
                rsqrt_act(act, m_var, m_r, ("pair seed", st, p))
                if p in (1, 3, 8):
                    split_hi(act)
            for n in range(HEADS + 2):
                if n < HEADS:
                    act.wait_ge(dve_did["minus max"], dve_did.at("minus max", st, n))
                    if n > 1:
                        act.wait_ge(pe_did["turned"], pe_did.at("turned", st, n - 2))
                    for j, s_ in enumerate((slice(0, P), slice(P, WIDE))):
                        last = nc.scalar.activation(m_p[:, n % 2, s_], Q[n % 2][:, s_], ACT.Exp, bias=small[:, 8 * (n % 2) + j:8 * (n % 2) + j + 1],
                                                    scale=QK_SCALE, accum_out=small[:, 8 * (n % 2) + 2 + j:8 * (n % 2) + 3 + j])
                    last.then_inc(act_did["exp"], act_did.next("exp", st, n))
                if 0 < n <= HEADS:
                    act.wait_ge(pe_did["turned"], pe_did.at("turned", st, n - 1))
                    if n > 2:
                        act.wait_ge(pe_did["values"], pe_did.at("values", st, n - 3))
                    nc.scalar.activation(m_pt[:, (n - 1) % 2, :], Q[2 + (n - 1) % 2][:, 0:WIDE], ACT.Copy).then_inc(
                        act_did["turned copy"], act_did.next("turned copy", st, n - 1))
                if n > 1 and n % 2:
                    round_c(act, st, n // 2 - 1, bank(Y[n // 2 - 1]), "pe", ("values", st, n - 2))
            for _ in range(4):
                split_hi(act)

        def mla_dve(dve, st):
            def v(ins):
                link(dve, "dve", ins)

            def mul(out, a_, b_):
                v(nc.vector.tensor_tensor(out, a_, b_, ALU.mult))

            for _ in range(4):
                split_lo(dve)
            rms_dve(dve, st, psum[7])
            for f in range(4):
                n = 2 if f < 3 else 1
                dve.wait_ge(pe_did["down"], pe_did.at("down", st, f))
                nc.vector.tensor_tensor(latent[:, 2 * f:2 * f + n, :], bank(psum[f])[:, 0:n, :],
                                                  rstd[:, :].unsqueeze(1).to_broadcast([P, n, T]), ALU.mult).then_inc(
                                                      dve_did["latent"], dve_did.next("latent", st, f))
            dve.wait_ge(pos_in, 16)
            v(nc.vector.tensor_copy(angle, positions[:, :]))
            v(nc.vector.tensor_scalar(angle, angle, column("inv_freq"), None, ALU.mult))
            reduce_angle(dve, angle, turns_, ("angle", st))
            dve.wait_ge(pe_did["latent sums"], pe_did.at("latent sums", st))
            for j, (src, width) in enumerate(((bank(psum[4])[:, 0, :], 384), (bank(psum[4])[:, 1, :], 256), (bank(psum[5])[:, 0, :], 64))):
                last = nc.vector.tensor_scalar(latent_var[:, j, :], src, 1.0 / width, NORM_EPS, ALU.mult, ALU.add)
            last.then_inc(dve_did["latent variance"], dve_did.next("latent variance", st))
            dve.wait_ge(act_did["latent seed"], act_did.at("latent seed", st))
            newton_dve(dve, latent_var, latent_r, latent_t)
            for c in range(7):
                name, i, j = ("q_norm", c, 0) if c < 3 else ("kv_norm", c - 3, 1) if c < 5 else ("kr", c - 5, 2)
                last = nc.vector.scalar_tensor_tensor(latent[:, c, :], latent[:, c, :], column(name, i), latent_r[:, j, :], ALU.mult, ALU.mult)
            last.then_inc(dve_did["latent normed"], dve_did.next("latent normed", st))
            dve.wait_ge(act_did["latent hi"], act_did.at("latent hi", st))
            nc.vector.tensor_tensor(c_lo[:, 0:5, :], latent[:, 0:5, :], c_hi[:, 0:5, :].bitcast(F32), ALU.subtract).then_inc(
                dve_did["latent lo"], dve_did.next("latent lo", st))
            dve.wait_ge(act_did["rotation"], act_did.at("rotation", st))
            k1, k2 = latent[:, 5, :], latent[:, 6, :]
            t = [tmp_r[:, :], tmp_n[:, :]]
            for half, (a_, b_, op) in enumerate(((k1, k2, ALU.subtract), (k2, k1, ALU.add))):
                mul(t[0], a_, cosine)
                mul(t[1], b_, sine)
                v(nc.vector.tensor_tensor(t[0], t[0], t[1], op))
                for j in range(4):
                    last = nc.vector.tensor_scalar(m_kr[:, j, half, :], t[0], column("head_mask", j), None, ALU.mult)
                v(last)
            split_lo(dve)
            for p in range(PAIRS):
                dve.wait_ge(pe_did["pair sums"], pe_did.at("pair sums", st, p))
                nc.vector.tensor_scalar(m_var, bank(m_bank(p, "sum")), 1.0 / (64 if p == 0 else P), NORM_EPS, ALU.mult, ALU.add).then_inc(
                    dve_did["pair variance"], dve_did.next("pair variance", st, p))
                dve.wait_ge(act_did["pair seed"], act_did.at("pair seed", st, p))
                newton_dve(dve, m_var, m_r, m_t)
                if p == 0:
                    n1, n2 = h1n[:, :, :], silu_h[:, :, :]
                    nc.vector.scalar_tensor_tensor(n1, bank(m_bank(0, "raw")), column("qr", 0), m_r, ALU.mult, ALU.mult)
                    nc.vector.scalar_tensor_tensor(n2, bank(m_bank(0, "raw2")), column("qr", 1), m_r, ALU.mult, ALU.mult).then_inc(
                        dve_did["normed pair"], dve_did.next("normed pair", st, 0))
                    dve.wait_ge(dve_did["normed pair"], dve_did.at("normed pair", st, 0))
                    for half, (a_, b_, op) in enumerate(((n1, n2, ALU.subtract), (n2, n1, ALU.add))):
                        mul(gated[:, :, :], a_, over_pair(cosine))
                        mul(h[:, :, :], b_, over_pair(sine))
                        last = nc.vector.tensor_tensor(m_qr[:, half, :, :], gated[:, :, :], h[:, :, :], op)
                        if half == 0:
                            v(last)
                    last.then_inc(dve_did["rope"], dve_did.next("rope", st))
                else:
                    dst, i, g = (m_q, p - 1, "qn") if p < 5 else (m_k, p - 5, "kn")
                    nc.vector.scalar_tensor_tensor(pair(dst, i), bank(m_bank(p, "raw")), column(g), m_r, ALU.mult, ALU.mult).then_inc(
                        dve_did["normed pair"], dve_did.next("normed pair", st, p))
                if p in (1, 3, 8):
                    split_lo(dve)
            for i in range(4):
                dve.wait_ge(pe_did["mla v"], pe_did.at("mla v", st, i))
                nc.vector.tensor_copy(m_v[:, i % 2, i // 2 * 512:(i // 2 + 1) * 512], psum[i][:, :]).then_inc(
                    dve_did["mla v copy"], dve_did.next("mla v copy", st, i))
            for n in range(HEADS + 2):
                if n < HEADS:
                    s8 = 8 * (n % 2)
                    dve.wait_ge(pe_did["scores"], pe_did.at("scores", st, n))
                    if n > 1:
                        dve.wait_ge(act_did["exp"], act_did.at("exp", st, n - 2))
                    nc.vector.tensor_reduce(small[:, s8:s8 + 1], Q[n % 2][:, 0:P], AX.X, ALU.max)
                    v(nc.vector.tensor_reduce(small[:, s8 + 1:s8 + 2], Q[n % 2][:, P:WIDE], AX.X, ALU.max))
                    nc.vector.tensor_scalar(small[:, s8:s8 + 2], small[:, s8:s8 + 2], -QK_SCALE, None, ALU.mult).then_inc(
                        dve_did["minus max"], dve_did.next("minus max", st, n))
                    dve.wait_ge(act_did["exp"], act_did.at("exp", st, n))
                    v(nc.vector.reciprocal(small[:, s8 + 4:s8 + 6], small[:, s8 + 2:s8 + 4]))
                    nc.vector.tensor_scalar(m_p[:, n % 2, 0:P], m_p[:, n % 2, 0:P], small[:, s8 + 4:s8 + 5], None, ALU.mult)
                    nc.vector.tensor_scalar(m_p[:, n % 2, P:WIDE], m_p[:, n % 2, P:WIDE], small[:, s8 + 5:s8 + 6], None, ALU.mult).then_inc(
                        dve_did["probabilities"], dve_did.next("probabilities", st, n))
                if n > 1 and n % 2:
                    rest_of_c(dve, st, n // 2 - 1, bank(Y[n // 2 - 1]))
            for _ in range(4):
                split_lo(dve)

        TILES_S, SPANS, SPAN = 16, 8, 32
        s5_u = region(0, 4, T)
        s5_v = region(1024, 4, T)
        s5_e = [region(2048 + 512 * i, TILES_S, SPAN) for i in range(2)]
        s5_f = [region(3072 + 512 * i, TILES_S, SPAN) for i in range(2)]
        s5_mag = region(4096, 2, 512)
        s5_b = region(5120, 4, 2, P)
        s5_c = [region(6144 + 512 * i, TILES_S, SPAN) for i in range(2)]
        s5_t = [region(11264 + 512 * i, 512) for i in range(4)]
        two_tiles = lambda at, step: scr[:, at:at + 2 * step].rearrange("p (n a) -> p n a", n=2)[:, :, 0:512]
        s5_turned = [[two_tiles(11264, 512), two_tiles(12288, 512)], [two_tiles(1024, 512), two_tiles(4096, 1024)]]
        s5_tanh = region(7168, 4, T)
        s5_out = region(8192, 4, T)
        sums = [hidden_buf[:, 0:4, :], hidden_buf[:, 4:8, :]]
        s5_r = scr[:, 7168:11264].rearrange("p (c q s j) -> p q s c j", c=SPANS, q=2, s=8)
        s5_s = [[h1n, silu_h, gated, h], [region(11264 + 512 * i, 2, T) for i in range(4)]]
        spans = lambda ap: ap.rearrange("p s (c j) -> p s c j", j=SPAN)

        def cols16(buf, i, n=1):
            return buf[:, 16 * i:16 * (i + n)]

        s5_dt, s5_m, s5_ang, s5_turns, s5_size, s5_sin, s5_cos, s5_tmp = (cols16(small, i) for i in range(8))
        lb_re, lb_im, s5_den, s5_num, f_re, f_im, s5_t2, e32_re, e32_im = (cols16(rstd, i) for i in range(9))
        minus_c_im = [tmp_r, tmp_n]
        carry = rstd[:, 192:256]

        s5_y_bank = [Y[0], Q[0]]

        def s5_pe(pe, st):
            product(pe, 8, KC, x_hi, x_lo, lambda n: (Y[n // 2], bank(Y[n // 2])[:, n % 2, :]),
                    lambda n: ("uv", st, n // 2) if n % 2 else None, input_ready(pe, st))
            for f in range(4):
                after(Y[f], ("act", ("uv", st, f)))

            def drive(p):
                if p in (0, 4):
                    pe.wait_ge(act_did["uv"], act_did.at("uv", st, p // 4))
                if p == 0:
                    pe.wait_ge(s5_in, 16)
                for s in (2 * p, 2 * p + 1):
                    b = Q[s % 4]
                    before(pe, b)
                    rows = slice(32 * (s % 4), 32 * (s % 4) + 32)
                    for part in range(2):
                        last = nc.tensor.matmul(bank(b)[:, part, :], s5_b[rows, s // 4, part, :], s5_u[rows, s // 4, :],
                                                start=True, stop=True, skip_group_check=True,
                                                tile_position=(32 * (s % 4), 0))
                    last.then_inc(pe_did["drive"], pe_did.next("drive", st, s))
                    after(b, ("dve", ("rotated", st, s)))

            def read_out(p):
                b = s5_y_bank[p // 4]
                if p % 4 == 0:
                    before(pe, b)
                    if p == 0:
                        pe.wait_ge(dve_did["minus c_im"], dve_did.at("minus c_im", st))
                pe.wait_ge(dve_did["states"], dve_did.at("states", st, p))
                pe.wait_ge(pool_did["states"], pool_did.at("states", st, p))
                for n in range(2):
                    s = 2 * p + n
                    rows = slice(32 * (s % 4), 32 * (s % 4) + 32)
                    minus = minus_c_im[s // 8][:, 32 * (s % 8):32 * (s % 8) + 32]
                    for q, c in enumerate((s5_c[0][:, s, :], s5_c[0][:, s, :], s5_c[1][:, s, :], minus)):
                        last = nc.tensor.matmul(bank(b)[rows, p // 2 % 2, :], c, s5_s[p % 2][q][:, n, :],
                                                start=(q == 0), stop=(q == 3), skip_group_check=True,
                                                tile_position=(0, 32 * (s % 4)))
                last.then_inc(pe_did["read out"], pe_did.next("read out", st, p))

            for p in range(6):
                drive(p)
            for n in range(4):
                pe.wait_ge(dve_did["pooled lo"], dve_did.at("pooled lo", st, n // 2))
                t, b = next_block(pe)
                hi, lo = block_of(t, b)
                if n % 2 == 0:
                    before(pe, Y[2 + n // 2])
                last = three(bank(Y[2 + n // 2])[:, n % 2, :], hi, lo, c_hi[:, 4 + n, :], c_lo[:, 4 + n, :], True, True)
                if n % 2:
                    last.then_inc(pe_did["pooled"], pe_did.next("pooled", st, n // 2))
                    after(Y[2 + n // 2], ("dve", ("pool out", st, n // 2)))
            for p in range(4):
                read_out(p)
            after(Y[0], ("dve", ("s5 y", st, 0)))
            for p in range(6, 8):
                drive(p)
            out = lambda n: (Y[n // 2], bank(Y[n // 2])[:, n % 2, :])
            for b in Y:
                before(pe, b)
                nc.tensor.matmul(b[:, :], zeros[:, 0:P], zeros[:, :], start=True, stop=False, skip_group_check=True)
            product(pe, KC, 4, c_hi[:, 4:8, :], c_lo[:, 4:8, :], out, lambda n: None,
                    lambda k: pe.wait_ge(dve_did["c_lo"], dve_did.at("c_lo", st, 2 + k // 2)), add=(False, False))
            for p in range(4, 8):
                read_out(p)
            after(Q[0], ("dve", ("s5 y", st, 1)))
            product(pe, 4, 4, c_hi, c_lo, lambda n: (Q[1 + n // 2], bank(Q[1 + n // 2])[:, n % 2, :]),
                    lambda n: ("glu", st, n // 2) if n % 2 else None,
                    lambda k: pe.wait_ge(dve_did["yg lo"], dve_did.at("yg lo", st, k // 2)))
            for i in range(2):
                after(Q[1 + i], ("act", ("glu", st, i)))
            product(pe, KC, 4, c_hi, c_lo, out, lambda n: ("y", st, n // 2) if n % 2 else None,
                    lambda k: pe.wait_ge(dve_did["c_lo"], dve_did.at("c_lo", st, k // 2)), add=(False, True))
            for i in range(4):
                after(Y[i], ("dve", ("z", st, i)))
            end_stream_stage(pe, st)

        def s5_setup_act(act, st):
            act.wait_ge(s5_par_in, 16)
            nc.scalar.activation(s5_dt, column("log_dt", 0, 16), ACT.Exp).then_inc(act_did["dt"], act_did.next("dt", st))
            act.wait_ge(dve_did["log mag"], dve_did.at("log mag", st))
            nc.scalar.activation(s5_m, s5_m, ACT.Exp).then_inc(act_did["mag"], act_did.next("mag", st))
            act.wait_ge(dve_did["theta"], dve_did.at("theta", st))
            sine_act(act, s5_ang, s5_size, s5_sin, s5_cos, ("sine", st))

        def s5_act(act, st):
            split_hi(act)
            for f in range(4):
                split_hi(act)
                act.wait_ge(pe_did["uv"], pe_did.at("uv", st, f))
                nc.scalar.activation(pair((s5_u, s5_v)[f // 2], f % 2), bank(Y[f]), ACT.Copy).then_inc(
                    act_did["uv"], act_did.next("uv", st, f))
            for i in range(2):
                act.wait_ge(dve_did["pooled"], dve_did.at("pooled", st, 3))
                for n in range(2):
                    last = nc.scalar.activation(c_hi[:, 4 + 2 * i + n, :], sums[n][:, 2 * i + n, :], ACT.Copy)
                last.then_inc(act_did["pooled hi"], act_did.next("pooled hi", st, i))
            act.wait_ge(pe_did["pooled"], pe_did.at("pooled", st, 1))
            for i in range(2):
                act.wait_ge(dve_did["pool out"], dve_did.at("pool out", st, i))
                nc.scalar.activation(pair(c_hi, 2 + i), pair(s5_v, i), ACT.Copy).then_inc(
                    act_did["c_hi"], act_did.next("c_hi", st, 2 + i))
            for i in range(2):
                if i:
                    split_hi(act)
                act.wait_ge(dve_did["s5 y"], dve_did.at("s5 y", st, i))
                link(act, "act", nc.scalar.activation(pair(s5_u, i), pair(s5_u, i), ACT.Gelu_apprx_tanh))
                nc.scalar.activation(pair(c_hi, i), pair(s5_u, i), ACT.Copy).then_inc(
                    act_did["yg hi"], act_did.next("yg hi", st, i))
            for i in range(2):
                act.wait_ge(pe_did["glu"], pe_did.at("glu", st, i))
                nc.scalar.activation(pair(s5_tanh, i), bank(Q[1 + i]), ACT.Tanh, scale=0.5).then_inc(
                    act_did["glu"], act_did.next("glu", st, i))
            for i in range(2):
                act.wait_ge(dve_did["gated y"], dve_did.at("gated y", st, i))
                nc.scalar.activation(pair(c_hi, i), pair(s5_out, i), ACT.Copy, scale=0.5).then_inc(
                    act_did["c_hi"], act_did.next("c_hi", st, i))
            for _ in range(4):
                split_hi(act)

        def complex_times(v, out, a_, b_, t, conjugate=False):
            tt = nc.vector.tensor_tensor
            tt(t[0], a_[0], b_[0], ALU.mult)
            tt(t[1], a_[1], b_[1], ALU.mult)
            tt(t[2], a_[0], b_[1], ALU.mult)
            v(tt(t[3], a_[1], b_[0], ALU.mult))
            tt(out[0], t[0], t[1], ALU.add if conjugate else ALU.subtract)
            v(tt(out[1], t[3], t[2], ALU.subtract if conjugate else ALU.add))

        lam_re, lam_im = column("lam_re", 0, 16), column("lam_im", 0, 16)
        tt, stt, ts = nc.vector.tensor_tensor, nc.vector.scalar_tensor_tensor, nc.vector.tensor_scalar
        s5_k = carry.rearrange("p (a to fr s) -> p a to fr s", a=2, to=2, fr=2)

        def s5_angles_dve(dve, st):
            def v(ins):
                link(dve, "dve", ins)

            dve.wait_ge(s5_par_in, 16)
            dve.wait_ge(act_did["dt"], act_did.at("dt", st))
            tt(s5_m, lam_re, s5_dt, ALU.mult).then_inc(dve_did["log mag"], dve_did.next("log mag", st))
            v(tt(s5_ang, lam_im, s5_dt, ALU.mult))
            reduce_angle(dve, s5_ang, s5_turns, ("theta", st))
            tt(s5_den, lam_re, lam_re, ALU.mult)
            v(tt(s5_t2, lam_im, lam_im, ALU.mult))
            v(tt(s5_den, s5_den, s5_t2, ALU.add))
            v(nc.vector.reciprocal(s5_den, s5_den))

        def s5_powers_dve(dve, st):
            def v(ins):
                link(dve, "dve", ins)

            for re, one in ((s5_e[0], 1.0), (s5_e[1], 0.0)):
                last = nc.vector.memset(re[:, :, 0:1], one)
            v(last)
            dve.wait_ge(act_did["mag"], act_did.at("mag", st))
            dve.wait_ge(act_did["sine"], act_did.at("sine", st))
            v(tt(lb_re, s5_m, s5_cos, ALU.mult))
            v(tt(lb_im, s5_m, s5_sin, ALU.mult))
            v(ts(s5_num, lb_re, -1.0, None, ALU.add))
            complex_times(v, (f_re, f_im), (s5_num, lb_im), (lam_re, lam_im), (s5_dt, s5_turns, s5_size, s5_tmp), conjugate=True)
            v(tt(f_re, f_re, s5_den, ALU.mult))
            v(tt(f_im, f_im, s5_den, ALU.mult))
            nc.vector.tensor_copy(s5_e[0][:, :, 1], s5_cos)
            v(ts(s5_e[1][:, :, 1], s5_sin, -1.0, None, ALU.mult))
            for m in (1, 2, 4, 8):
                double(v, m)

        def double(v, m):
            n = min(m, SPAN - 1 - m)
            at = [t[:, 0:16 * n].rearrange("p (s j) -> p s j", j=n) for t in s5_t]
            complex_times(v, [e[:, :, m + 1:m + 1 + n] for e in s5_e], [e[:, :, 1:1 + n] for e in s5_e],
                          [e[:, :, m:m + 1].to_broadcast([P, TILES_S, n]) for e in s5_e], at)

        def s5_dve(dve, st):
            def v(ins):
                link(dve, "dve", ins)

            split_lo(dve)
            double(v, 16)
            complex_times(v, (e32_re, e32_im), [e[:, :, 16] for e in s5_e], [e[:, :, 16] for e in s5_e],
                          (s5_dt, s5_turns, s5_size, s5_tmp))
            over_j = lambda ap: ap.unsqueeze(2).to_broadcast([P, TILES_S, SPAN])
            complex_times(v, s5_f, (over_j(f_re), over_j(f_im)), s5_e,
                          [t.rearrange("p (s j) -> p s j", j=SPAN) for t in s5_t])
            k = s5_k
            by_half = lambda ap: ap.rearrange("p (a s) -> p a s", a=2)
            for to, fr, e in ((0, 0, e32_re), (1, 1, e32_re), (0, 1, e32_im)):
                last = tt(k[:, :, to, fr, :], by_half(e), by_half(s5_m), ALU.mult)
            v(stt(k[:, :, 1, 0, :], by_half(e32_im), -1.0, by_half(s5_m), ALU.mult, ALU.mult))
            split_lo(dve)
            mag = s5_mag.rearrange("p a (q s j) -> p a q s j", q=2, s=8)
            for half in range(2):
                for q in range(2):
                    last = nc.vector.tensor_copy(mag[:, half, q, :, :], s5_m[:, 8 * half:8 * half + 8].unsqueeze(2).to_broadcast([P, 8, SPAN]))
            v(last)
            v(nc.vector.memset(s5_mag.rearrange("p a (n j) -> p (a n) j", j=SPAN)[:, :, 0:1], 0.0))
            dve.wait_ge(s5_in, 16)
            for half in range(2):
                last = ts(minus_c_im[half][:, :], scr[:, 6656 + 256 * half:6912 + 256 * half], -1.0, None, ALU.mult)
            last.then_inc(dve_did["minus c_im"], dve_did.next("minus c_im", st))
            split_lo(dve)
            split_lo(dve)

            def rotate(p):
                by_f, by_fi = s5_turned[p // 4]
                for n in range(2):
                    s = 2 * p + n
                    dve.wait_ge(pe_did["drive"], pe_did.at("drive", st, s))
                    drive = bank(Q[s % 4]).rearrange("p q (c j) -> p q c j", j=SPAN)
                    for out, f, in ((by_f, s5_f[0]), (by_fi, s5_f[1])):
                        last = tt(out[:, n, :].rearrange("p (q c j) -> p q c j", q=2, j=SPAN), drive,
                                  f[:, s, :].unsqueeze(1).unsqueeze(1).to_broadcast([P, 2, SPANS, SPAN]), ALU.mult)
                    last.then_inc(dve_did["rotated"], dve_did.next("rotated", st, s))
                dve.wait_ge(dve_did["rotated"], dve_did.at("rotated", st, 2 * p + 1))
                if p >= 4:
                    dve.wait_ge(pool_did["states"], pool_did.at("states", st, p - 4))
                tiles = slice(2 * (p % 4), 2 * (p % 4) + 2)
                re, im = ([spans(by[:, :, T * part:T * part + T]) for by in (by_f, by_fi)] for part in range(2))
                tt(s5_r[:, 0, tiles], re[0], im[1], ALU.subtract)
                tt(s5_r[:, 1, tiles], im[0], re[1], ALU.add).then_inc(dve_did["r"], dve_did.next("r", st, p))
                dve.wait_ge(dve_did["r"], dve_did.at("r", st, p))

            def scan(half):
                moved = var[:, 0:32].rearrange("p (to fr s) -> p to fr s", to=2, fr=2)
                for c in range(SPANS):
                    flat = scr[:, 7168 + 512 * c:7168 + 512 * (c + 1)]
                    ins = nc.vector.tensor_tensor_scan(flat, s5_mag[:, half, :], flat, 0.0, ALU.mult, ALU.add)
                    if c == SPANS - 1:
                        ins.then_inc(dve_did["scanned"], dve_did.next("scanned", st, half))
                        dve.wait_ge(dve_did["scanned"], dve_did.at("scanned", st, half))
                    else:
                        v(ins)
                        v(tt(moved, k[:, half], s5_r[:, :, :, c, SPAN - 1].unsqueeze(1).to_broadcast([P, 2, 2, 8]), ALU.mult))
                        first = s5_r[:, :, :, c + 1, 0]
                        v(tt(first, first, moved[:, :, 0, :], ALU.add))
                        v(tt(first, first, moved[:, :, 1, :], ALU.add))

            def states(p):
                if p == 0:
                    dve.wait_ge(act_did["pooled hi"], act_did.at("pooled hi", st, 1))
                    dve.wait_ge(dve_did["pooled lo"], dve_did.at("pooled lo", st, 1))
                if p >= 2:
                    dve.wait_ge(pe_did["read out"], pe_did.at("read out", st, p - 2))
                tiles = slice(2 * (p % 4), 2 * (p % 4) + 2)
                er, ei = (e[:, 2 * p:2 * p + 2, :].unsqueeze(2).to_broadcast([P, 2, SPANS, SPAN]) for e in s5_e)
                tt(spans(s5_s[p % 2][0]), s5_r[:, 0, tiles], er, ALU.mult)
                tt(spans(s5_s[p % 2][1]), s5_r[:, 1, tiles], ei, ALU.mult).then_inc(
                    dve_did["states"], dve_did.next("states", st, p))

            def add_skip(i):
                dve.wait_ge(pe_did["read out"], pe_did.at("read out", st, 4 * i + 3))
                for c in (2 * i, 2 * i + 1):
                    last = stt(s5_u[:, c, :], s5_u[:, c, :], column("s5_d", c), bank(s5_y_bank[i])[:, c % 2, :], ALU.mult, ALU.add)
                last.then_inc(dve_did["s5 y"], dve_did.next("s5 y", st, i))

            for p in range(4):
                rotate(p)
            dve.wait_ge(pool_did["window sums"], pool_did.at("window sums", st))
            for g in range(4):
                w = 2 ** (g + 1)
                stt(sums[g % 2][:, g, :], sums[g % 2][:, g, :], 1.0 / w, s5_v[:, g, :], ALU.mult, ALU.subtract).then_inc(
                    dve_did["pooled"], dve_did.next("pooled", st, g))
            scan(0)
            split_lo(dve)
            for i in range(2):
                dve.wait_ge(act_did["pooled hi"], act_did.at("pooled hi", st, i))
                for n in range(2):
                    g = 2 * i + n
                    last = tt(c_lo[:, 4 + g, :], sums[n][:, g, :], c_hi[:, 4 + g, :].bitcast(F32), ALU.subtract)
                last.then_inc(dve_did["pooled lo"], dve_did.next("pooled lo", st, i))
            for p in range(4):
                states(p)
            for p in range(4, 8):
                rotate(p)
            for i in range(2):
                dve.wait_ge(pe_did["pooled"], pe_did.at("pooled", st, i))
                tt(pair(s5_v, i), bank(Y[2 + i]), over_tokens(column("pool_scale", 2 * i, 2)), ALU.mult).then_inc(
                    dve_did["pool out"], dve_did.next("pool out", st, i))
            add_skip(0)
            for i in range(2):
                rest_of_c(dve, st, 2 + i, pair(s5_v, i))
            scan(1)
            for p in range(4, 8):
                states(p)
            split_lo(dve)
            for i in range(2):
                if i:
                    add_skip(1)
                dve.wait_ge(act_did["yg hi"], act_did.at("yg hi", st, i))
                tt(pair(c_lo, i), pair(s5_u, i), pair(c_hi, i).bitcast(F32), ALU.subtract).then_inc(
                    dve_did["yg lo"], dve_did.next("yg lo", st, i))
            for i in range(2):
                dve.wait_ge(act_did["glu"], act_did.at("glu", st, i))
                stt(pair(s5_out, i), pair(s5_tanh, i), 1.0, pair(s5_u, i), ALU.add, ALU.mult).then_inc(
                    dve_did["gated y"], dve_did.next("gated y", st, i))
            for i in range(2):
                dve.wait_ge(act_did["c_hi"], act_did.at("c_hi", st, i))
                stt(pair(c_lo, i), pair(s5_out, i), 0.5, pair(c_hi, i).bitcast(F32), ALU.mult, ALU.subtract).then_inc(
                    dve_did["c_lo"], dve_did.next("c_lo", st, i))
            for _ in range(4):
                split_lo(dve)

        def s5_pool(pool, st):
            def v(ins):
                link(pool, "pool", ins)

            pool.wait_ge(act_did["uv"], act_did.at("uv", st, 3))
            src = s5_v
            for level in range(4):
                w, dst, g = 2 ** level, sums[level % 2], slice(level, 4)
                nc.gpsimd.tensor_copy(dst[:, g, 0:w], src[:, g, 0:w])
                v(nc.gpsimd.tensor_tensor(dst[:, g, w:], src[:, g, w:], src[:, g, 0:T - w], ALU.add))
                src = dst
            count = column("pool_count", 0, 64).rearrange("p (g t) -> p g t", t=16)
            for g in range(4):
                last = nc.gpsimd.tensor_tensor(sums[g % 2][:, g, 0:16], sums[g % 2][:, g, 0:16], count[:, g, :], ALU.mult)
            last.then_inc(pool_did["window sums"], pool_did.next("window sums", st))
            for p in range(8):
                if p % 4 == 0:
                    pool.wait_ge(dve_did["scanned"], dve_did.at("scanned", st, p // 4))
                if p == 0:
                    pool.wait_ge(act_did["pooled hi"], act_did.at("pooled hi", st, 1))
                    pool.wait_ge(dve_did["pooled lo"], dve_did.at("pooled lo", st, 1))
                if p >= 2:
                    pool.wait_ge(pe_did["read out"], pe_did.at("read out", st, p - 2))
                tiles = slice(2 * (p % 4), 2 * (p % 4) + 2)
                er, ei = (e[:, 2 * p:2 * p + 2, :].unsqueeze(2).to_broadcast([P, 2, SPANS, SPAN]) for e in s5_e)
                nc.gpsimd.tensor_tensor(spans(s5_s[p % 2][2]), s5_r[:, 0, tiles], ei, ALU.mult)
                nc.gpsimd.tensor_tensor(spans(s5_s[p % 2][3]), s5_r[:, 1, tiles], er, ALU.mult).then_inc(
                    pool_did["states"], pool_did.next("states", st, p))

        block = ctx.enter_context(nc.Block())

        @block.sync
        def _(sp):
            sp.dma_start(x[:, :, :], dram["x"]).then_inc(x_in, 16)
            for i in range(RING):
                sp.dma_start(raw[:, i, :], dram["stream"][i]).then_inc(raw_in[i], 16)
            with sp.Fori(1, n_tiles // RING) as r:
                for i in range(RING):
                    sp.wait_ge(lo_done, r * RING + (i + 1 - RING))
                    sp.dma_start(raw[:, i, :], dram["stream"][bass.DynSlice(r * RING + i, 1)]
                                 .rearrange("a p n -> (a p) n")).then_inc(raw_in[i], 16)
            for i in range(4):
                sp.wait_ge(dve_did["x"], dve_did.at("x", len(stages) - 1, i))
                sp.dma_start(dram["out"][:, i, :], pair(x, i)).then_inc(out_done, 16)
            sp.wait_ge(out_done, 64)
            for i in range(RING):
                sp.wait_ge(raw_in[i], 16 * (n_tiles // RING))

        @block.gpsimd
        def _(pool):
            pool.dma_start(region(0, 4, T), dram["ple"]).then_inc(p_in, 16)
            pool.dma_start(scr[:, 5120:7168], dram["s5"]).then_inc(s5_in, 16)
            pool.dma_start(positions[:, :], dram["positions"].to_broadcast([P, T])).then_inc(pos_in, 16)
            nc.gpsimd.memset(ones[:, :], 1.0).then_inc(pool_did["ones"], pool_did.next("ones"))
            nc.gpsimd.memset(zeros[:, :], 0.0).then_inc(pool_did["zeros"], pool_did.next("zeros"))
            for st, s in enumerate(stages):
                if s[0] == "s5":
                    s5_pool(pool, st)

        @block.scalar
        def _(act):
            early = columns["ln_mix_g"]
            act.dma_start(par[:, 0:early], dram["par"][:, 0:early]).then_inc(s5_par_in, 16)
            act.dma_start(par[:, early:], dram["par"][:, early:]).then_inc(par_in, 16)
            if stages[0][0] == "s5":
                s5_setup_act(act, 0)
            act.wait_ge(x_in, 16)
            feed_act(act, -1)
            split_hi(act)
            split_hi(act)
            act.wait_ge(p_in, 16)
            nc.scalar.activation(p_hi[:, :, :], region(0, 4, T), ACT.Copy).then_inc(act_did["p_hi"], act_did.next("p_hi"))
            act.wait_ge(dve_did["p_lo"], dve_did.at("p_lo"))
            for st, s in enumerate(stages):
                settle(act, "act")
                if s[0] == "s5":
                    s5_act(act, st)
                if s[0] == "moe":
                    moe_act(act, st)
                if s[0] == "sb":
                    sb_act(act, st)
                if s[0] == "conv":
                    conv_act(act, st)
                if s[0] == "lru":
                    lru_act(act, st)
                if s[0] == "mla":
                    mla_act(act, st)
                if s[0] in ("moe", "ffn"):
                    ffn_act(act, st)
                close_act(act, st)

        @block.vector
        def _(dve):
            if stages[0][0] == "s5":
                s5_angles_dve(dve, 0)
            dve.wait_ge(x_in, 16)
            dve.wait_ge(par_in, 16)
            for i in range(5):
                feed_dve(dve, -1, i)
            if stages[0][0] == "s5":
                s5_powers_dve(dve, 0)
            split_lo(dve)
            split_lo(dve)
            dve.wait_ge(act_did["p_hi"], act_did.at("p_hi"))
            nc.vector.tensor_tensor(p_lo[:, :, :], region(0, 4, T), p_hi[:, :, :].bitcast(F32), ALU.subtract).then_inc(
                dve_did["p_lo"], dve_did.next("p_lo"))
            for st, s in enumerate(stages):
                settle(dve, "dve")
                if s[0] == "s5":
                    s5_dve(dve, st)
                if s[0] == "moe":
                    moe_dve(dve, st)
                if s[0] == "sb":
                    sb_dve(dve, st)
                if s[0] == "conv":
                    conv_dve(dve, st)
                if s[0] == "lru":
                    lru_dve(dve, st)
                if s[0] == "mla":
                    mla_dve(dve, st)
                if s[0] in ("moe", "ffn"):
                    ffn_dve(dve, st)
                close_dve(dve, st)

        @block.tensor
        def _(pe):
            pe.wait_ge(pool_did["ones"], pool_did.at("ones"))
            pe.wait_ge(pool_did["zeros"], pool_did.at("zeros"))
            for st, s in enumerate(stages):
                if s[0] == "s5":
                    s5_pe(pe, st)
                if s[0] == "moe":
                    moe_pe(pe, st)
                if s[0] == "sb":
                    sb_pe(pe, st)
                if s[0] == "conv":
                    conv_pe(pe, st)
                if s[0] == "lru":
                    lru_pe(pe, st)
                if s[0] == "mla":
                    mla_pe(pe, st)
                if s[0] in ("moe", "ffn"):
                    ffn_pe(pe, st)
                close_pe(pe, st)
    return {who: d.new for who, d in did.items()}


def blocks(w):
    k, n = w.shape
    return w.reshape(k // P, P, n // P, P).transpose(2, 0, 1, 3).reshape(-1, P, P)


def chunks(v):
    return np.ascontiguousarray(v.reshape(-1, P).T)


def ffn_blocks(w1, w3, w2):
    units = w1.shape[1] // UNIT
    one = [blocks(w1[:, u * UNIT:(u + 1) * UNIT]) for u in range(units)]
    three_ = [blocks(w3[:, u * UNIT:(u + 1) * UNIT]) for u in range(units)]
    two = [blocks(w2[u * UNIT:(u + 1) * UNIT]) for u in range(units)]
    out = [one[0], three_[0]]
    for s in range(units - 1):
        out += [one[s + 1], three_[s + 1], two[s]]
    return out + [two[units - 1]]


def param_columns():
    widths = dict(lam_re=16, lam_im=16, log_dt=16, half_pi=1, ln_mix_g=16, ln_mix_b=16, ln_ffn_g=16, ln_ffn_b=16, mix_norm=32, ffn_norm=32,
                  router_w=128, router_bias=16, s5_d=4, pool_scale=4,
                  pool_count=64, conv_w=48, lru_conv_w=40, lru_conv_b=10, lru_ba=10, lru_bx=10,
                  lru_lam=10, q_norm=3, kv_norm=2, qn=1, qr=2, kn=1, kr=2, inv_freq=1, head_mask=4,
                  order=20, ident=128, minus_tri=128, minus_ones=128, strict=128, future=128, causal=128, quarter=128)
    columns, at = {}, 0
    for name, width in widths.items():
        columns[name] = at
        at += width
    columns["total"] = at
    return columns


def kernel(**inputs):
    import concourse.bacc as bacc
    from concourse.bass_utils import run_bass_kernel_spmd as run

    a = {name: np.asarray(v) for name, v in inputs.items()}
    columns = param_columns()
    par = np.zeros((P, columns["total"]), np.float32)

    def put(name, value):
        par[:, columns[name]:columns[name] + value.shape[1]] = value

    p = np.arange(P)
    put("pool_count", np.tile(np.concatenate([w / np.minimum(np.arange(16) + 1, w) for w in (2, 4, 8, 16)])
                              .astype(np.float32)[None], (P, 1)))
    put("inv_freq", (np.float32(10000.0) ** (-np.arange(0, 64, 2, dtype=np.float32) / np.float32(64)))[p % 32][:, None])
    put("half_pi", np.full((P, 1), np.pi / 2, np.float32))
    put("head_mask", (p[:, None] // 32 == np.arange(4)[None]).astype(np.float32))
    put("order", np.tile(np.concatenate([np.arange(4, 0, -1), np.arange(16, 0, -1)]).astype(np.float32)[None], (P, 1)))
    put("ident", np.eye(P, dtype=np.float32))
    put("minus_tri", -(p[:, None] >= p[None]).astype(np.float32))
    put("minus_ones", -np.ones((P, P), np.float32))
    put("future", np.where(p[:, None] < p[None], 0.0, -NEG).astype(np.float32))
    put("strict", (p[:, None] < p[None]).astype(np.float32))
    put("causal", np.where(p[None] <= p[:, None], 0.0, -NEG).astype(np.float32))
    put("quarter", (p[:, None] // 32 == p[None] // 32).astype(np.float32))

    for name in ("ln_mix_g", "ln_mix_b", "ln_ffn_g", "ln_ffn_b"):
        put(name, chunks(a[name]))
    put("mix_norm", chunks(a["mix_norm_2"]))
    put("ffn_norm", chunks(a["ffn_norm_2"]))
    put("router_w", a["router_w"].reshape(KC, P, N_EXPERTS).transpose(1, 0, 2).reshape(P, -1))
    put("router_bias", np.tile(a["router_bias"][None], (P, 1)))
    put("lam_re", chunks(a["s5_lambda_re"]))
    put("lam_im", chunks(a["s5_lambda_im"]))
    put("log_dt", chunks(np.repeat(a["s5_log_dt"][0], 64)))
    put("s5_d", chunks(a["s5_d"]))
    put("pool_scale", chunks(a["pool_scale"]))
    put("conv_w", chunks(a["conv_w_2"]))
    put("lru_conv_w", chunks(a["lru_conv_w_2"]))
    put("lru_conv_b", chunks(a["lru_conv_b_2"]))
    put("lru_ba", chunks(a["lru_gate_a_b_2"]))
    put("lru_bx", chunks(a["lru_gate_x_b_2"]))
    put("lru_lam", chunks(a["lru_lambda_2"]))
    put("q_norm", chunks(a["mla_q_norm_2"]))
    put("kv_norm", chunks(a["mla_kv_norm_2"]))
    put("qn", chunks(a["mla_qn_norm_2"]))
    put("kn", chunks(a["mla_kn_norm_2"]))
    put("qr", np.tile(a["mla_qr_norm_2"].reshape(2, 32).T, (4, 1)))
    put("kr", np.tile(a["mla_kr_norm_2"].reshape(2, 32).T, (4, 1)))

    s5_b = np.zeros((4, 2, 16, 4, 2, 2, 64), np.float32)
    s5_c = np.zeros((2, 64, 2, 16, 2, 16), np.float32)
    for i, name in enumerate(("s5_b_re", "s5_b_im")):
        b = a[name][0].reshape(4, 4, 2, 64, 16)
        for g in range(2):
            s5_b[:, g, :, :, i, g, :] = b[:, :, g].transpose(1, 3, 0, 2)
    for i, name in enumerate(("s5_c_re", "s5_c_im")):
        c = a[name][0].reshape(16, 2, 16, 64)
        for g in range(2):
            s5_c[g, :, i, :, g, :] = c[:, g].transpose(2, 0, 1)

    stream = []
    for stage in STAGES:
        kind = stage[0]
        if kind == "ffn":
            w = a["ffn_w_gu_2"][stage[1]]
            parts = ffn_blocks(w[:, :D_FF], w[:, D_FF:], a["ffn_w_down_2"][stage[1]])
        elif kind == "moe":
            w1, w3 = (a[n][stage[1]].transpose(1, 0, 2).reshape(D, -1) for n in ("moe_w1", "moe_w3"))
            parts = [blocks(a["ple_w_proj"][stage[1]]), blocks(a["ple_w_gate"][stage[1]])]
            parts += ffn_blocks(w1, w3, a["moe_w2"][stage[1]].reshape(-1, D))
        elif kind == "s5":
            w = a["ab_w_out"][0]
            parts = [blocks(a["ab_w_in"][0])] + [blocks(w_) for w_ in a["pool_w"][0]]
            parts += [blocks(w[512:]), blocks(a["s5_w_glu"][0]), blocks(w[:512])]
        elif kind == "sb":
            w = a["sb_w_qkv"][0]
            v = w[:, 2 * D:].reshape(KC, P, 2, 4, P).transpose(2, 0, 3, 1, 4).reshape(-1, P, P)
            parts = [blocks(w[:, :2 * D]), v, blocks(a["sb_w_out"][0])]
        elif kind == "conv":
            w = a["conv_w_in_2"][stage[1]].reshape(D, 3, 4, UNIT)
            parts = [blocks(w[:, j, i]) for i in range(4) for j in (1, 2, 0)] + [blocks(a["conv_w_out_2"][stage[1]])]
        elif kind == "lru":
            w = blocks(a["lru_w_in_2"][0])
            inner = np.stack([a["lru_gate_a_w_2"][0].reshape(5, 2, P, P), a["lru_gate_x_w_2"][0].reshape(5, 2, P, P)], 1)
            parts = [w[80:], w[:16], inner.reshape(-1, P, P), w[16:80], blocks(a["lru_w_out_2"][0])]
        elif kind == "mla":
            w = a["mla_w_down_2"][0]
            rope = [np.tile(w[:, 640 + 32 * i:672 + 32 * i], (1, 4)) for i in range(2)]
            q = a["mla_w_uq_2"][0].reshape(384, 8, 192)
            kv = a["mla_w_ukv_2"][0].reshape(256, 8, 256)
            v = np.ascontiguousarray(kv[:, :, 128:]).reshape(2, P, 2, 4, P).transpose(2, 0, 3, 1, 4).reshape(-1, P, P)
            parts = [blocks(w[:, :640])] + [blocks(r) for r in rope]
            parts += [blocks(np.ascontiguousarray(q[:, :, 128:160]).reshape(384, -1)), blocks(np.ascontiguousarray(q[:, :, 160:]).reshape(384, -1))]
            parts += [blocks(np.ascontiguousarray(q[:, :, :128]).reshape(384, -1)), blocks(np.ascontiguousarray(kv[:, :, :128]).reshape(256, -1)), v]
            parts += [blocks(a["mla_w_o_2"][0])]
        n = sum(len(q_) for q_ in parts)
        assert n == stage_blocks(stage), (stage, n, stage_blocks(stage))
        stream += parts + [np.zeros((-n % BLOCKS_PER_TILE, P, P), np.float32)]
    _, n_tiles = stream_plan(STAGES)
    have = sum(len(q_) for q_ in stream)
    stream.append(np.zeros((n_tiles * BLOCKS_PER_TILE - have, P, P), np.float32))
    stream = np.concatenate(stream).reshape(n_tiles, BLOCKS_PER_TILE, P, P).transpose(0, 2, 1, 3).reshape(n_tiles, P, TILE)

    arrays = {
        "x": np.ascontiguousarray(a["x"][0].reshape(T, KC, P).transpose(2, 1, 0)),
        "ple": np.ascontiguousarray(a["p"][:, 0].reshape(2, T, 2, P).transpose(3, 0, 2, 1).reshape(P, 4, T)),
        "positions": np.ascontiguousarray(a["positions_2"].reshape(1, T)),
        "par": par,
        "s5": np.concatenate([s5_b.reshape(P, 1024), s5_c.reshape(P, 1024)], 1),
        "stream": np.ascontiguousarray(stream),
    }

    def program(known):
        nc = bacc.Bacc("TRN2", target_bir_lowering=False, num_devices=1)
        dram = {name: nc.dram_tensor(f"in_{name}", v.shape, mybir.dt.from_np(v.dtype), kind="ExternalInput").ap()
                for name, v in arrays.items()}
        dram["out"] = nc.dram_tensor("out_x", (P, 4, 2, T), F32, kind="ExternalOutput").ap()
        return nc, build(nc, dram, columns, STAGES, known)

    _, known = program(None)
    nc, again = program(known)
    assert again == known
    r = run(nc, [{f"in_{name}": v for name, v in arrays.items()}], core_ids=[0]).results[0]["out_x"]
    return np.ascontiguousarray(r.reshape(P, KC, T).transpose(2, 1, 0)).reshape(1, T, D)
```
